# Optimizing a Trainium2 kernel written in Bass

```python
import jax, jax.numpy as jnp
from jax import lax
import numpy as np

D_MODEL = 1024
BATCH = 1
SEQ = 1024
DEPTH = 1
DEC_BATCH = 1
DEC_SEQ = 64
PAST_LEN = 512

CHUNK = 64
Q_BLOCK = 128
N_MEM = 256
EPS = 1e-6
BRANCH_W = D_MODEL // 2
N_BRANCH = 3
SB_HEADS = 8
SB_DIM = BRANCH_W // SB_HEADS
SB_W = SB_HEADS * SB_DIM
GLA_HEADS = 4
GLA_DK = 64
GLA_DV = BRANCH_W // GLA_HEADS
GLA_K = GLA_HEADS * GLA_DK
GLA_V = GLA_HEADS * GLA_DV
GLA_RANK = 16
GLA_TAU = 16.0
MEM_HEADS = 4
MEM_DIM = BRANCH_W // MEM_HEADS
MEM_W = MEM_HEADS * MEM_DIM
SPLITS = (SB_W, SB_W, SB_W, GLA_K, GLA_K, GLA_V, GLA_RANK, GLA_V, MEM_W, N_BRANCH * D_MODEL)
IN_W = SB_W * 3 + GLA_K * 2 + GLA_V * 2 + GLA_RANK + MEM_W + N_BRANCH * D_MODEL
N_GROUPS = 4
EXPERTS_PER_GROUP = 8
N_EXPERTS = N_GROUPS * EXPERTS_PER_GROUP
TOP_K = 2
D_EXPERT = D_MODEL // 2
MOE_BLOCK = 128

kernel_name = 'hybrid_stream_sb_gla_hmoe_step'

def rmsnorm(x, g):
    x32 = x.astype(jnp.float32)
    y = x32 * lax.rsqrt(jnp.mean(x32 * x32, axis=-1, keepdims=True) + EPS)
    return (y * g.astype(jnp.float32)).astype(x.dtype)

def mix_projections(x, g, w_in, w_a2, b_a):
    B, T, _ = x.shape
    u = rmsnorm(x, g) @ w_in
    sq, sk, sv, gq, gk, gv, glr, gr, mq, gt = jnp.split(u, np.cumsum(SPLITS)[:-1].tolist(), axis=-1)
    log_a = jax.nn.log_sigmoid((glr @ w_a2 + b_a).astype(jnp.float32)) / GLA_TAU
    hd = lambda a, h: a.reshape(B, T, h, -1)
    return (hd(sq, SB_HEADS), hd(sk, SB_HEADS), hd(sv, SB_HEADS),
            hd(gq, GLA_HEADS) * GLA_DK ** -0.5, hd(gk, GLA_HEADS), hd(gv, GLA_HEADS),
            hd(log_a, GLA_HEADS), gr, hd(mq, MEM_HEADS), gt.reshape(B, T, N_BRANCH, D_MODEL))

def sb_attend(q, k, v, q_pos, k_pos):
    f32 = jnp.float32
    z = jnp.einsum('bqhd,bkhd->bhqk', q.astype(f32), k.astype(f32)) * SB_DIM ** -0.5
    mask = k_pos[None, :] < q_pos[:, None]
    log_1mb = jnp.where(mask, jax.nn.log_sigmoid(-z), 0.0)
    after = lax.cumsum(log_1mb, axis=3, reverse=True) - log_1mb
    att = jnp.where(mask, jnp.exp(jax.nn.log_sigmoid(z) + after), 0.0)
    return jnp.einsum('bhqk,bkhd->bqhd', att, v.astype(f32)).astype(v.dtype)

def sb_prompt(q, k, v):
    T = q.shape[1]
    outs = []
    for i0 in range(0, T, Q_BLOCK):
        i1 = min(i0 + Q_BLOCK, T)
        outs.append(sb_attend(q[:, i0:i1], k[:, :i1], v[:, :i1], jnp.arange(i0, i1), jnp.arange(i1)))
    return jnp.concatenate(outs, axis=1)

def sb_sample(q, k, v, ck, cv):
    P, T = ck.shape[1], q.shape[1]
    kk = jnp.concatenate([ck.astype(k.dtype), k], axis=1)
    vv = jnp.concatenate([cv.astype(v.dtype), v], axis=1)
    return sb_attend(q, kk, vv, P + jnp.arange(T), jnp.arange(P + T))

def gla_chunked(q, k, v, log_a, S0, chunk):
    B, T, H, _ = q.shape
    n = T // chunk
    f32 = jnp.float32
    def blk(a):
        return a.astype(f32).reshape(B, n, chunk, H, a.shape[-1]).transpose(1, 0, 3, 2, 4)
    q, k, v, la = blk(q), blk(k), blk(v), blk(log_a)
    b = jnp.cumsum(la, axis=3)
    b_last = b[:, :, :, -1:, :]
    q_d = q * jnp.exp(b)
    k_d = k * jnp.exp(-b)
    k_e = k * jnp.exp(b_last - b)
    causal = jnp.tril(jnp.ones((chunk, chunk), bool))
    att = jnp.where(causal, jnp.einsum('nbhid,nbhjd->nbhij', q_d, k_d), 0.0)
    o_intra = jnp.einsum('nbhij,nbhjv->nbhiv', att, v)
    def step(S, xs):
        qd, ke, vv, bl = xs
        o = jnp.einsum('bhid,bhdv->bhiv', qd, S)
        S = jnp.exp(bl[:, :, 0, :])[..., None] * S + jnp.einsum('bhjd,bhjv->bhdv', ke, vv)
        return S, o
    S_fin, o_inter = lax.scan(step, S0.astype(f32), (q_d, k_e, v, b_last))
    o = (o_intra + o_inter).transpose(1, 0, 3, 2, 4).reshape(B, T, H, v.shape[-1])
    return o, S_fin

def gla_out(o, gr, g):
    B, T, H, DV = o.shape
    on = o * lax.rsqrt(jnp.mean(o * o, axis=-1, keepdims=True) + EPS) * g.astype(jnp.float32).reshape(H, DV)
    return (on.reshape(B, T, H * DV) * jax.nn.silu(gr.astype(jnp.float32))).astype(gr.dtype)

def memory_kv(mem, g, w):
    B, M, _ = mem.shape
    mk, mv = jnp.split(rmsnorm(mem, g) @ w, 2, axis=-1)
    return mk.reshape(B, M, MEM_HEADS, MEM_DIM), mv.reshape(B, M, MEM_HEADS, MEM_DIM)

def memory_attend(q, mk, mv):
    B, T = q.shape[:2]
    s = jnp.einsum('bqhd,bmhd->bhqm', q.astype(jnp.float32), mk.astype(jnp.float32)) * MEM_DIM ** -0.5
    p = jax.nn.softmax(s, axis=-1)
    o = jnp.einsum('bhqm,bmhd->bqhd', p, mv.astype(jnp.float32))
    return o.reshape(B, T, MEM_W).astype(q.dtype)

def merge_branches(x, o_sb, o_gla, o_mem, gates, w_branch, w_out):
    B, T, _ = x.shape
    o = jnp.stack([o_sb.reshape(B, T, SB_W), o_gla, o_mem], axis=2)
    p = jnp.einsum('btnc,ncd->btnd', o, w_branch)
    mixed = jnp.sum(jax.nn.sigmoid(gates) * p, axis=2)
    return x + mixed @ w_out

def hier_route(xt, w_coarse, b_coarse, w_fine, b_fine):
    lc = (xt @ w_coarse + b_coarse).astype(jnp.float32)
    pc = jax.nn.softmax(lc, axis=-1)
    p_grp, grp = lax.top_k(pc, 1)
    lf_all = jnp.einsum('td,gde->tge', xt, w_fine) + b_fine
    lf = jnp.take_along_axis(lf_all, grp[:, :, None], axis=1)[:, 0].astype(jnp.float32)
    pf = jax.nn.softmax(lf, axis=-1)
    topv, topi = lax.top_k(pf, TOP_K)
    topv = topv / jnp.sum(topv, axis=-1, keepdims=True)
    return grp * EXPERTS_PER_GROUP + topi, p_grp * topv

def moe_experts(xt, expert_idx, weights, wg, wu, wd):
    T, D = xt.shape
    A = T * TOP_K
    flat_e = expert_idx.reshape(A)
    flat_t = jnp.repeat(jnp.arange(T), TOP_K)
    flat_w = weights.reshape(A)
    order = jnp.argsort(flat_e)
    se = flat_e[order]
    counts = jnp.bincount(flat_e, length=N_EXPERTS)
    padded = (counts + MOE_BLOCK - 1) // MOE_BLOCK * MOE_BLOCK
    start = jnp.cumsum(counts) - counts
    pend = jnp.cumsum(padded)
    pstart = pend - padded
    dest = pstart[se] + jnp.arange(A) - start[se]
    n_blk = -(-(A + N_EXPERTS * (MOE_BLOCK - 1)) // MOE_BLOCK)
    P = n_blk * MOE_BLOCK
    tok_buf = jnp.full((P,), T, jnp.int32).at[dest].set(flat_t[order])
    w_buf = jnp.zeros((P,), xt.dtype).at[dest].set(flat_w[order].astype(xt.dtype))
    blk_e = jnp.minimum(jnp.searchsorted(pend, jnp.arange(n_blk) * MOE_BLOCK, side='right'), N_EXPERTS - 1)
    xpad = jnp.concatenate([xt, jnp.zeros((1, D), xt.dtype)], axis=0)
    xb = xpad[tok_buf].reshape(n_blk, MOE_BLOCK, D)
    def expert_block(args):
        xblk, e = args
        return (jax.nn.silu(xblk @ wg[e]) * (xblk @ wu[e])) @ wd[e]
    yb = lax.map(expert_block, (xb, blk_e))
    y = jnp.zeros((T + 1, D), xt.dtype).at[tok_buf].add(yb.reshape(P, D) * w_buf[:, None])
    return y[:T]

def channel_mixer(h, g, w_coarse, b_coarse, w_fine, b_fine, wg, wu, wd):
    B, T, D = h.shape
    ht = rmsnorm(h, g).reshape(B * T, D)
    idx, wts = hier_route(ht, w_coarse, b_coarse, w_fine, b_fine)
    return h + moe_experts(ht, idx, wts, wg, wu, wd).reshape(B, T, D)

def setup_inputs(seed: int = 0) -> dict:
    key = jax.random.key(seed)
    ks = jax.random.split(key, 26)
    f32 = jnp.float32
    nrm = lambda k, shape, scale: jax.random.normal(k, shape, f32) * scale
    gain = lambda k, shape: 1.0 + 0.01 * jax.random.normal(k, shape, f32)
    L, D = DEPTH, D_MODEL
    return {
        'x_prompt': nrm(ks[0], (BATCH, SEQ, D), 1.0),
        'x_sample': nrm(ks[1], (DEC_BATCH, DEC_SEQ, D), 1.0),
        'mem_prompt': nrm(ks[2], (BATCH, N_MEM, D), 1.0),
        'cache_sb_k': nrm(ks[3], (L, DEC_BATCH, PAST_LEN, SB_HEADS, SB_DIM), 1.0),
        'cache_sb_v': nrm(ks[4], (L, DEC_BATCH, PAST_LEN, SB_HEADS, SB_DIM), 1.0),
        'state_gla': nrm(ks[5], (L, DEC_BATCH, GLA_HEADS, GLA_DK, GLA_DV), 1.0),
        'cache_mem_k': nrm(ks[6], (L, DEC_BATCH, N_MEM, MEM_HEADS, MEM_DIM), 1.0),
        'cache_mem_v': nrm(ks[7], (L, DEC_BATCH, N_MEM, MEM_HEADS, MEM_DIM), 1.0),
        'norm_mix': gain(ks[8], (L, D)),
        'w_in': nrm(ks[9], (L, D, IN_W), D ** -0.5),
        'w_gla_a2': nrm(ks[10], (L, GLA_RANK, GLA_K), GLA_RANK ** -0.5),
        'b_gla_a': nrm(ks[11], (L, GLA_K), 0.02),
        'gla_norm': gain(ks[12], (L, GLA_V)),
        'norm_mem': gain(ks[13], (L, D)),
        'w_mem_kv': nrm(ks[14], (L, D, 2 * MEM_W), D ** -0.5),
        'w_branch': nrm(ks[15], (L, N_BRANCH, BRANCH_W, D), BRANCH_W ** -0.5),
        'w_out': nrm(ks[16], (L, D, D), D ** -0.5),
        'norm_ffn': gain(ks[17], (L, D)),
        'w_coarse': nrm(ks[18], (L, D, N_GROUPS), D ** -0.5),
        'b_coarse': nrm(ks[19], (L, N_GROUPS), 0.01),
        'w_fine': nrm(ks[20], (L, N_GROUPS, D, EXPERTS_PER_GROUP), D ** -0.5),
        'b_fine': nrm(ks[21], (L, N_GROUPS, EXPERTS_PER_GROUP), 0.01),
        'w_e_gate': nrm(ks[22], (L, N_EXPERTS, D, D_EXPERT), D ** -0.5),
        'w_e_up': nrm(ks[23], (L, N_EXPERTS, D, D_EXPERT), D ** -0.5),
        'w_e_down': nrm(ks[24], (L, N_EXPERTS, D_EXPERT, D), D_EXPERT ** -0.5),
        'norm_final': gain(ks[25], (D,)),
    }

def reference(x_prompt, x_sample, mem_prompt, cache_sb_k, cache_sb_v, state_gla, cache_mem_k, cache_mem_v,
              norm_mix, w_in, w_gla_a2, b_gla_a, gla_norm, norm_mem, w_mem_kv, w_branch, w_out,
              norm_ffn, w_coarse, b_coarse, w_fine, b_fine, w_e_gate, w_e_up, w_e_down, norm_final):
    hp, hs = x_prompt, x_sample
    sbk_p, sbv_p, gla_p, mk_p, mv_p = [], [], [], [], []
    sbk_s, sbv_s, gla_s = [], [], []
    for l in range(DEPTH):
        ffn_w = (norm_ffn[l], w_coarse[l], b_coarse[l], w_fine[l], b_fine[l], w_e_gate[l], w_e_up[l], w_e_down[l])
        sq, sk, sv, gq, gk, gv, la, gr, mq, gt = mix_projections(hp, norm_mix[l], w_in[l], w_gla_a2[l], b_gla_a[l])
        s0 = jnp.zeros((hp.shape[0], GLA_HEADS, GLA_DK, GLA_DV), jnp.float32)
        o_gla, s_p = gla_chunked(gq, gk, gv, la, s0, CHUNK)
        mk, mv = memory_kv(mem_prompt, norm_mem[l], w_mem_kv[l])
        hp = merge_branches(hp, sb_prompt(sq, sk, sv), gla_out(o_gla, gr, gla_norm[l]),
                            memory_attend(mq, mk, mv), gt, w_branch[l], w_out[l])
        hp = channel_mixer(hp, *ffn_w)
        sbk_p.append(sk); sbv_p.append(sv); gla_p.append(s_p.astype(hp.dtype)); mk_p.append(mk); mv_p.append(mv)
        sq, sk, sv, gq, gk, gv, la, gr, mq, gt = mix_projections(hs, norm_mix[l], w_in[l], w_gla_a2[l], b_gla_a[l])
        o_gla, s_s = gla_chunked(gq, gk, gv, la, state_gla[l], hs.shape[1])
        hs = merge_branches(hs, sb_sample(sq, sk, sv, cache_sb_k[l], cache_sb_v[l]), gla_out(o_gla, gr, gla_norm[l]),
                            memory_attend(mq, cache_mem_k[l], cache_mem_v[l]), gt, w_branch[l], w_out[l])
        hs = channel_mixer(hs, *ffn_w)
        sbk_s.append(sk); sbv_s.append(sv); gla_s.append(s_s.astype(hs.dtype))
    y_prompt = rmsnorm(hp, norm_final)
    y_sample = rmsnorm(hs, norm_final)
    sb_k_prompt, sb_v_prompt = jnp.stack(sbk_p), jnp.stack(sbv_p)
    gla_state_prompt = jnp.stack(gla_p)
    mem_k_prompt, mem_v_prompt = jnp.stack(mk_p), jnp.stack(mv_p)
    sb_k_sample, sb_v_sample = jnp.stack(sbk_s), jnp.stack(sbv_s)
    gla_state_sample = jnp.stack(gla_s)
    return (y_prompt, y_sample, sb_k_prompt, sb_v_prompt, gla_state_prompt, mem_k_prompt, mem_v_prompt,
            sb_k_sample, sb_v_sample, gla_state_sample)


_drawn_inputs = setup_inputs


def setup_inputs(seed=0):
    import zlib

    import numpy as np

    out = dict(_drawn_inputs(seed))
    spreads = {}
    factors = {'norm_mix': 3.097,
     'b_gla_a': 6.477,
     'gla_norm': 23.818,
     'norm_mem': 14.981,
     'b_fine': 25.016,
     'norm_final': 174.377,
     'cache_sb_k': 23.055,
     'cache_sb_v': 8.771,
     'norm_ffn': 8.0,
     'b_coarse': 8.0}
    for name, (base, spread) in spreads.items():
        noise = np.random.default_rng([zlib.crc32(name.encode()), seed]).standard_normal(out[name].shape)
        drawn = base * np.exp(spread * noise) if base else spread * noise
        out[name] = __import__('jax').numpy.asarray(drawn.astype(out[name].dtype))
    for name, factor in factors.items():
        out[name] = (out[name] * factor).astype(out[name].dtype)
    return out
```

```python
from contextlib import ExitStack

import concourse.bass as bass
from concourse import mybir

F32 = mybir.dt.float32
F32R = mybir.dt.float32r
I32 = mybir.dt.int32
U32 = mybir.dt.uint32
ACT = mybir.ActivationFunctionType
ALU = mybir.AluOpType
AX = mybir.AxisListType

P = 128
D = 1024
KC = D // P
SEQ, DEC = 1024, 64
T = SEQ + DEC
NT = 9
FULL = SEQ // P
GROUPS = [(0, 384), (384, 384), (768, 320)]
WIDE = [(0, 512), (512, 512), (1024, 64)]
PAST, NMEM, CH = 512, 256, 64
EPS = 1e-6
SBH, SBD = 8, 64
BW = 512
C_SQ, C_SK, C_SV = 0, 512, 1024
C_GQ, C_GK, C_GV = 1536, 1792, 2048
C_LR, C_GR, C_MQ, C_GT = 2560, 2576, 3088, 3600
RANK, TAU = 16, 16.0
NG, EPG, NE = 4, 8, 32
DE = 512
MAIN = 128
OVER = (2 * T) // (MAIN + 1)
SLOTS = (NE + OVER) * P


def rows_of(t):
    return P if t < FULL else DEC


class Stage(ExitStack):

    def __init__(self, nc):
        super().__init__()
        self.nc, self.held = nc, []
        self.callback(self.clear)

    def semaphore(self, name):
        self.held.append(self.nc.alloc_semaphore(name=name))
        return self.held[-1]

    def clear(self):
        self.nc.clear_and_free_semaphores(self.held)
        self.nc.all_engine_barrier()


class Stream:

    def __init__(self, nc, ctx, name, groups, wst, whi, wlo):
        self.nc, self.groups = nc, groups
        self.wst, self.whi, self.wlo = wst, whi, wlo
        self.nb = len(groups)
        self.per = sum(groups)
        s = lambda n: ctx.semaphore(f"{name}_{n}")
        self.loaded = [s(f"loaded{i}") for i in range(3)]
        self.high, self.low = s("high"), s("low")
        self.product, self.drained, self.passed = s("product"), s("drained"), s("passed")

    def end(self, j):
        return sum(self.groups[:j + 1])

    def load(self, sp, it, j, src):
        sp.wait_ge(self.low, self.nb * it + j + 1)
        sp.sem_inc(self.passed, 1)
        sp.dma_start(self.wst[j % 3][:, :, :], src).then_inc(self.loaded[j % 3], 16)

    def split_high(self, act, it, j):
        act.wait_ge(self.loaded[j % 3], 16 * (self.nb // 3 * it + j // 3 + 1))
        before = self.end(j - 3) + self.per if j >= 3 else self.end(j + self.nb - 3)
        act.wait_ge(self.product, self.per * it + before)
        self.nc.scalar.activation(self.whi[j % 3][:, :, :], self.wst[j % 3][:, :, :], ACT.Copy).then_inc(self.high, 1)

    def split_low(self, ve, it, j):
        ve.wait_ge(self.high, self.nb * it + j + 1)
        self.nc.vector.tensor_tensor(self.wlo[j % 3][:, :, :], self.wst[j % 3][:, :, :],
                                     self.whi[j % 3][:, :, :].bitcast(F32), ALU.subtract).then_inc(self.low, 1)

    def project(self, pe, it, j, xhi, xlo, groups, banks, only=None):
        pe.wait_ge(self.low, self.nb * it + j + 4)
        for g, (c0, n) in enumerate(groups):
            if only is not None and g != only:
                continue
            pe.wait_ge(self.drained, self.per * it + self.end(j - 1) + g + 1)
            three_pass(self.nc, banks[g][:, 0:n], [
                (self.whi[j % 3][:, k, :], self.wlo[j % 3][:, k, :], xhi[:, k, c0:c0 + n], xlo[:, k, c0:c0 + n])
                for k in range(KC)]).then_inc(self.product, 1)

    def drain(self, act, it, j, g):
        act.wait_ge(self.product, self.per * (it + 1) + self.end(j - 1) + g + 1)


def three_pass(nc, out, parts):
    for i, (wh, wl, xh, xl) in enumerate(parts):
        nc.tensor.matmul(out, wl, xh, start=(i == 0), stop=False)
        nc.tensor.matmul(out, wh, xl, start=False, stop=False)
        last = nc.tensor.matmul(out, wh, xh, start=False, stop=(i == len(parts) - 1))
    return last


def build(nc, io, stop_after=99):
    top = ExitStack()
    xp = io["x_prompt"].rearrange("b t d -> (b t) d")
    xs = io["x_sample"].rearrange("b t d -> (b t) d")
    w_in = io["w_in"][0, :, :]
    w_in_k = w_in.rearrange("(k p) n -> p k n", p=P)
    htd = nc.dram_tensor("ffn_rows", (T, D), F32).ap()
    ysd = nc.dram_tensor("expert_rows", (SLOTS, D), F32).ap()
    slot_tok = nc.dram_tensor("slot_token", (SLOTS + 2 * P, 1), I32).ap()

    uid = [0]

    def at(name, shape, dt, off):
        uid[0] += 1
        return nc.alloc_sbuf_tensor_at(f"{name}_{uid[0]}", shape, dt, offset=BASE + off)

    BASE = 16512
    psum = [top.enter_context(nc.psum_tensor(f"bank{i}", [P, 512], F32)) for i in range(8)]
    PA, PB, TB, Z0, Z1, A0, A1, OB = psum

    TW = T * 4
    XH, XL = 0, KC * TW
    OS = 2 * KC * TW
    OG, OM = OS + 4 * TW, OS + 8 * TW
    RING = OS + 12 * TW
    CON = RING + 9 * 4096
    R2 = CON + 4096
    END = 212800
    xhi = at("xhi", [P, KC, T], F32R, XH)
    xlo = at("xlo", [P, KC, T], F32R, XL)
    o_sb = at("o_sb", [P, 4, T], F32, OS)
    o_gla = at("o_gla", [P, 4, T], F32, OG)
    o_mem = at("o_mem", [P, 4, T], F32, OM)
    wst = [at("wst", [P, KC, P], F32, RING + 4096 * i) for i in range(3)]
    whi = [at("whi", [P, KC, P], F32R, RING + 4096 * (3 + i)) for i in range(3)]
    wlo = [at("wlo", [P, KC, P], F32R, RING + 4096 * (6 + i)) for i in range(3)]
    ident = at("ident", [P, P], F32, CON)
    below = at("below", [P, P], F32, CON + 512)
    above = at("above", [P, P], F32, CON + 1024)
    ones = at("ones", [P, P], F32, CON + 1536)
    stat = at("stat", [P, 64], F32, CON + 2048)
    nbias = at("nbias", [P, 64], F32, CON + 2304)
    glrT = at("glrT", [P, T], F32, R2)
    R3 = R2 + TW

    def sems(ctx, prefix, names):
        return [ctx.semaphore(f"{prefix}_{n}") for n in names.split()]

    def norm_block(tag, tiles, gain, hi, lo, off, first):
        with Stage(nc) as ctx:
            xt = [at("xt", [P, D], F32, off + 4096 * i) for i in range(2)]
            xn = [at("xn", [P, D], F32, off + 8192 + 4096 * i) for i in range(2)]
            sq = at("sq", [P, D], F32, off + 16384)
            gb = at("gb", [P, D], F32, off + 20480)
            *loaded, gain_in, const, squared, inverted, rooted, normed, turned, high, low = sems(
                ctx, tag, "loaded0 loaded1 gain_in const squared inverted rooted normed turned high low")
            banks = [PA, PB, TB, Z0]
            loops = (len(tiles) // 2) if first else 0

            def each(eng, body):
                if loops:
                    with eng.Fori(0, FULL // 2) as i:
                        for u in range(2):
                            body(i * 2 + u, i, u, P, None)
                    n0 = FULL
                else:
                    n0 = 0
                for n in range(n0, len(tiles)):
                    body(n, n // 2, n % 2, tiles[n][1], tiles[n])

            def skewed(eng, norm, spread):
                at_ = lambda n: (n, n // 2, n % 2, tiles[n][1], tiles[n])
                norm(*at_(0))
                if loops:
                    with eng.Fori(0, FULL // 2 - 1) as i:
                        norm(i * 2 + 1, i, 1, P, None)
                        spread(i * 2, i, 0, P, None)
                        norm(i * 2 + 2, i + 1, 0, P, None)
                        spread(i * 2 + 1, i, 1, P, None)
                for n in range(FULL - 1 if loops else 1, len(tiles)):
                    norm(*at_(n))
                    spread(*at_(n - 1))
                spread(*at_(len(tiles) - 1))

            block = ctx.enter_context(nc.Block())

            @block.sync
            def _(sp):
                sp.dma_start(gb[:, :], gain.partition_broadcast(P)).then_inc(gain_in, 16)

                def body(n, turn, u, rows, tile):
                    sp.wait_ge(normed, n + 1)
                    src = tile[0] if tile else xp[bass.ds(n * P, P), :]
                    sp.dma_start(xt[u][0:rows, :], src).then_inc(loaded[u], 16)
                each(sp, body)

            @block.gpsimd
            def _(pool):
                if first:
                    nc.gpsimd.memset(ones[:, :], 1.0)
                    nc.gpsimd.memset(ident[:, :], 0.0)
                    pool.drain()
                    nc.gpsimd.affine_select(out=ident[:, :], in_=ident[:, :], compare_op=ALU.not_equal, fill=1.0,
                                            base=0, pattern=[[-1, P]], channel_multiplier=1)
                    nc.gpsimd.affine_select(out=below[:, :], in_=ones[:, :], compare_op=ALU.is_gt, fill=0.0,
                                            base=0, pattern=[[-1, P]], channel_multiplier=1)
                    nc.gpsimd.affine_select(out=above[:, :], in_=ones[:, :], compare_op=ALU.is_gt, fill=0.0,
                                            base=0, pattern=[[1, P]], channel_multiplier=-1)
                    pool.drain()
                pool.sem_inc(const, 1)

            @block.scalar
            def _(act):
                def body(n, turn, u, rows, tile):
                    act.wait_ge(loaded[u], turn * 16 + 16)
                    act.wait_ge(normed, n + 2)
                    nc.scalar.activation(sq[0:rows, :], xt[u][0:rows, :], ACT.Square,
                                         scale=D ** -0.5, accum_out=stat[0:rows, 0:1]).then_inc(squared, 1)
                    act.wait_ge(inverted, n + 1)
                    nc.scalar.activation(stat[0:rows, 2:3], stat[0:rows, 1:2], ACT.Sqrt).then_inc(rooted, 1)

                def spread(n, turn, u, rows, tile):
                    for q in range(2):
                        b = banks[2 * u + q]
                        act.wait_ge(turned, 2 * n + q + 1)
                        c0 = n * P if first else tile[2]
                        dst = hi[:, 4 * q:4 * q + 4, bass.ds(c0, rows)]
                        nc.scalar.activation(dst, b[:, :].rearrange("p (k t) -> p k t", k=4)[:, :, 0:rows],
                                             ACT.Copy).then_inc(high, 1)
                skewed(act, body, spread)

            @block.vector
            def _(ve):
                ve.sem_inc(normed, 2)
                ve.sem_inc(low, 4)
                ve.wait_ge(gain_in, 16)

                def body(n, turn, u, rows, tile):
                    ve.wait_ge(squared, n + 1)
                    nc.vector.tensor_scalar(stat[0:rows, 1:2], stat[0:rows, 0:1], EPS, None, ALU.add)
                    ve.drain()
                    nc.vector.reciprocal(stat[0:rows, 1:2], stat[0:rows, 1:2]).then_inc(inverted, 1)
                    ve.wait_ge(rooted, n + 1)
                    nc.vector.scalar_tensor_tensor(out=xn[u][0:rows, :], in0=xt[u][0:rows, :],
                                                   scalar=stat[0:rows, 2:3], in1=gb[0:rows, :],
                                                   op0=ALU.mult, op1=ALU.mult).then_inc(normed, 1)

                def spread(n, turn, u, rows, tile):
                    for q in range(2):
                        b = banks[2 * u + q]
                        ve.wait_ge(high, 2 * n + q + 1)
                        c0 = n * P if first else tile[2]
                        cols = bass.ds(c0, rows)
                        nc.vector.tensor_tensor(lo[:, 4 * q:4 * q + 4, cols],
                                                b[:, :].rearrange("p (k t) -> p k t", k=4)[:, :, 0:rows],
                                                hi[:, 4 * q:4 * q + 4, cols].bitcast(F32),
                                                ALU.subtract).then_inc(low, 1)
                skewed(ve, body, spread)

            @block.tensor
            def _(pe):
                pe.wait_ge(const, 1)

                def body(n, turn, u, rows, tile):
                    pe.wait_ge(normed, n + 3)
                    for q in range(2):
                        pe.wait_ge(low, 2 * n + q + 1)
                        for k in range(4):
                            kk = 4 * q + k
                            last = nc.tensor.transpose(banks[2 * u + q][:, k * P:k * P + rows],
                                                       xn[u][0:rows, kk * P:(kk + 1) * P], ident[0:rows, 0:rows])
                        last.then_inc(turned, 1)
                each(pe, body)

    norm_block("a", [(None, P, None)] * FULL + [(xs[:, :], DEC, SEQ)],
               io["norm_mix"][0, :], xhi, xlo, R3, True)

    qT = at("qT", [P, T], F32, OG)
    kT = at("kT", [P, T], F32, OG + TW)
    vT = at("vT", [P, T], F32, OG + 2 * TW)
    kn = at("kn", [P, NT, P], F32, OG + 3 * TW)
    vn = at("vn", [P, NT, P], F32, OG + 3 * TW + 4608)
    lsum = [at("lsum", [P, 512], F32, OG + 3 * TW + 9216 + 2048 * i) for i in range(2)]
    qs = at("qs", [P, 4, DEC], F32, OG + 3 * TW + 9216 + 4096)
    ks = at("ks", [P, 4, DEC], F32, OG + 3 * TW + 9216 + 5120)
    vs = at("vs", [P, BW], F32, OG + 3 * TW + 9216 + 6144)
    assert 3 * TW + 9216 + 8192 <= 8 * TW
    lnb = [at("lnb", [P, 512], F32, R3 + 2048 * i) for i in range(4)]
    L = [at("L", [P, 512], F32, R3 + 2048 * (4 + i)) for i in range(4)]
    mb = [at("mb", [P, 512], F32, R3 + 2048 * (8 + i)) for i in range(4)]
    att = [at("att", [P, 512], F32, R3 + 2048 * (12 + i)) for i in range(2)]
    SCR = R3 + 2048 * 14
    ZB = [Z0, Z1, TB]

    steps = []
    for half in (1, 0):
        for j in range(4 * half + 3, -1, -1):
            for u in range(2):
                steps.append((half, j, u, max(j * P - half * 512, 0)))
    NS = len(steps)
    diag = [j >= 4 * half for half, j, u, lo in steps]
    nd = [sum(diag[:s]) for s in range(NS + 1)]
    SPLITS = [6, 10, 14]
    first_of = [s for s in range(NS) if s == 0 or steps[s][0] != steps[s - 1][0]]
    with Stage(nc) as ctx:
        st = Stream(nc, ctx, "b", [3, 3, 3], wst, whi, wlo)
        turned, copied, stored, scored, logged, split, masked, summed, subbed, weighed, cut, used, added, \
            out_read, passed = sems(ctx, "sb", "turned copied stored scored logged split masked summed subbed "
                            "weighed cut used added out_read passed")
        block = ctx.enter_context(nc.Block())
        kout = io["out2"].rearrange("l b t h d -> (l b t) (h d)").rearrange("(n p) c -> p n c", p=P)
        vout = io["out3"].rearrange("l b t h d -> (l b t) (h d)").rearrange("(n p) c -> p n c", p=P)
        kouts = io["out7"].rearrange("l b t h d -> (l b t) (h d)")
        vouts = io["out8"].rearrange("l b t h d -> (l b t) (h d)")
        pbanks = [PA, PB, OB]

        @block.sync
        def _(sp):
            sp.sem_inc(stored, 64)
            for j, c0 in enumerate((C_SQ, C_SK, C_SV)):
                st.load(sp, 0, j, w_in_k[:, :, c0:c0 + P])
            with sp.Fori(0, 4) as hp:
                with sp.If(hp < 3):
                    for j, c0 in enumerate((C_SQ, C_SK, C_SV)):
                        st.load(sp, hp + 1, j, w_in_k[:, :, bass.ds(c0 + (hp + 1) * P, P)])
                with sp.If(hp > 2):
                    st.load(sp, 4, 0, w_in_k[:, :, C_LR:C_LR + P])
                for q, (nat, dst, dsts) in enumerate(((kn, kout, kouts), (vn, vout, vouts))):
                    sp.wait_ge(copied, 6 * hp + 3 * q + 6)
                    sp.dma_start(dst[:, :, bass.ds(hp * P, P)], nat[:, 0:FULL, :]).then_inc(stored, 16)
                    sp.dma_start(dsts[:, bass.ds(hp * P, P)], nat[0:DEC, FULL, :]).then_inc(stored, 16)
            sp.wait_ge(stored, 64 * 5)

        @block.tensor
        def _(pe):
            pe.sem_inc(st.product, st.per)
            pe.sem_inc(used, 2)
            st.project(pe, 0, 0, xhi, xlo, GROUPS, pbanks, only=0)
            st.project(pe, 0, 0, xhi, xlo, GROUPS, pbanks, only=1)
            with pe.Fori(0, 4) as hp:
                def score(i):
                    half, j, u, lo = steps[i]
                    pe.wait_ge(split, NS * hp + i + 1)
                    nc.tensor.matmul(ZB[i % 3][:, lo:512], kT[u * 64:u * 64 + 64, j * P:(j + 1) * P],
                                     qT[u * 64:u * 64 + 64, half * 512 + lo:half * 512 + 512],
                                     start=True, stop=True).then_inc(scored, 1)

                def turn(q, src):
                    pe.wait_ge(st.drained, 9 * hp + 3 + 3 * q + 6)
                    for g in range(3):
                        pe.wait_ge(copied, 6 * hp + 3 * q + g + 1)
                        for t in range(3 * g, 3 * g + 3):
                            r = rows_of(t)
                            last = nc.tensor.transpose([TB, A0, A1][g][0:r, (t % 3) * P:(t % 3 + 1) * P],
                                                       src[:, t * P:t * P + r], ident[:, :])
                        last.then_inc(turned, 1)
                pe.wait_ge(out_read, 2 * hp + 1)
                st.project(pe, hp, 0, xhi, xlo, GROUPS, pbanks, only=2)
                st.project(pe, hp, 1, xhi, xlo, GROUPS, pbanks)
                st.project(pe, hp, 2, xhi, xlo, GROUPS, pbanks, only=0)
                pe.wait_ge(st.drained, 9 * hp + 3 + 6)
                score(0)
                score(1)
                st.project(pe, hp, 2, xhi, xlo, GROUPS, pbanks, only=1)
                turn(0, kT)
                st.project(pe, hp, 2, xhi, xlo, GROUPS, pbanks, only=2)
                turn(1, vT)
                pe.wait_ge(copied, 6 * hp + 9)
                for i in range(2, NS + 5):
                    if i < NS:
                        score(i)
                    if 3 <= i < NS + 3:
                        a = i - 3
                        half, j, u, lo = steps[a]
                        if diag[a]:
                            pe.wait_ge(masked, nd[NS] * hp + nd[a] + 1)
                        else:
                            pe.wait_ge(split, NS * hp + a + 4)
                        pe.wait_ge(subbed, NS * hp + a + 1)
                        A = [A0, A1][a % 2]
                        more = lo + P if diag[a] else lo
                        last = nc.tensor.matmul(A[:, lo:512], below[:, :], L[a % 4][:, lo:512],
                                                start=True, stop=(more == 512))
                        if more < 512:
                            pe.wait_ge(added, NS * hp + a + 3)
                            last = nc.tensor.matmul(A[:, more:512], ones[:, :], lsum[u][:, more:512],
                                                    start=False, stop=True)
                        last.then_inc(summed, 1)
                    if i in (NS + 1, NS + 3):
                        st.project(pe, hp + 1, 0, xhi, xlo, GROUPS, pbanks, only=(i - NS) // 2)
                    if i >= 5:
                        a = i - 5
                        half, j, u, lo = steps[a]
                        if diag[a]:
                            pe.wait_ge(cut, nd[NS] * hp + nd[a] + 1)
                        else:
                            pe.wait_ge(weighed, NS * hp + a + 5)
                        if a in first_of:
                            pe.wait_ge(out_read, 2 * hp + first_of.index(a) + 1)
                        nc.tensor.matmul(OB[u * 64:u * 64 + 64, lo:512], vn[:, j, u * 64:u * 64 + 64],
                                         att[a % 2][:, lo:512], start=(a in first_of or a - 1 in first_of),
                                         stop=(j == 0), skip_group_check=True).then_inc(used, 1)
            pe.wait_ge(out_read, 9)
            st.project(pe, 4, 0, xhi, xlo, GROUPS, pbanks, only=2)

        @block.scalar
        def _(act):
            nc.scalar.preload_act_table_set("natural_log_exp_and_others")
            act.sem_inc(st.drained, 3)
            act.sem_inc(weighed, 4)
            for j in range(3):
                st.split_high(act, 0, j)

            def logs(hp, i):
                half, j, u, lo = steps[i]
                b = lnb[i % 4]
                act.wait_ge(scored, NS * hp + i + 1)
                nc.scalar.activation(b[:, lo:512], ZB[i % 3][:, lo:512], ACT.Abs)
                act.drain()
                nc.scalar.activation(b[:, lo:512], b[:, lo:512], ACT.Exp, scale=-1.0)
                act.drain()
                nc.scalar.activation(b[:, lo:512], b[:, lo:512], ACT.Ln, bias=1.0).then_inc(logged, 1)

            def drain(hp, j, dst, scale, groups=range(3)):
                for g in groups:
                    c0, n = GROUPS[g]
                    st.drain(act, hp, j, g)
                    nc.scalar.activation(dst[:, c0:c0 + n], pbanks[g][:, 0:n], ACT.Copy,
                                         scale=scale).then_inc(st.drained, 1)
            with act.Fori(0, 4) as hp:
                drain(hp, 0, qT, SBD ** -0.5)
                drain(hp, 1, kT, 1.0)
                drain(hp, 2, vT, 1.0, [0])
                logs(hp, 0)
                logs(hp, 1)
                drain(hp, 2, vT, 1.0, [1, 2])
                for i in range(NS + 4):
                    if i == SPLITS[0]:
                        st.split_high(act, hp + 1, 0)
                    elif i in SPLITS:
                        with act.If(hp < 3):
                            st.split_high(act, hp + 1, SPLITS.index(i))
                    if 2 <= i < NS:
                        logs(hp, i)
                    if i >= 4:
                        a = i - 4
                        half, j, u, lo = steps[a]
                        act.wait_ge(subbed, NS * hp + a + 3)
                        act.wait_ge(used, NS * hp + a + 1)
                        nc.scalar.activation(att[a % 2][:, lo:512], mb[a % 4][:, lo:512],
                                             ACT.Exp).then_inc(weighed, 1)
            drain(4, 0, glrT, 1.0)

        @block.vector
        def _(ve):
            ve.sem_inc(st.low, 3)
            ve.sem_inc(copied, 3)
            ve.sem_inc(split, 3)
            ve.sem_inc(subbed, 2)
            ve.sem_inc(out_read, 1)
            for j in range(3):
                st.split_low(ve, 0, j)
            with ve.Fori(0, 4) as hp:
                ve.wait_ge(stored, 64 * hp + 64)
                for q, dst in enumerate((kn, vn)):
                    for g in range(3):
                        ve.wait_ge(turned, 6 * hp + 3 * q + g + 1)
                        full = min(3, FULL - 3 * g)
                        last = nc.vector.tensor_copy(dst[:, 3 * g:3 * g + full, :].rearrange("p a b -> p (a b)"),
                                                     [TB, A0, A1][g][:, 0:full * P])
                        if full < 3:
                            last = nc.vector.tensor_copy(dst[0:DEC, FULL, :], [TB, A0, A1][g][0:DEC, full * P:full * P + P])
                        last.then_inc(copied, 1)
                nc.vector.tensor_copy(qs[:, hp, :], qT[:, SEQ:T])
                nc.vector.tensor_copy(ks[:, hp, :], kT[:, SEQ:T])
                ve.drain()
                nc.vector.tensor_copy(vs[0:DEC, bass.ds(hp * P, P)], vn[0:DEC, FULL, :])
                for i in range(NS + 5):
                    if i == SPLITS[0]:
                        st.split_low(ve, hp + 1, 0)
                    elif i in SPLITS:
                        with ve.If(hp < 3):
                            st.split_low(ve, hp + 1, SPLITS.index(i))
                    if 2 <= i < NS + 2:
                        a = i - 2
                        half, j, u, lo = steps[a]
                        Z = ZB[a % 3]
                        ve.wait_ge(logged, NS * hp + a + 1)
                        ve.wait_ge(added, NS * hp + a + 1)
                        nc.vector.scalar_tensor_tensor(out=L[a % 4][:, lo:512], in0=Z[:, lo:512], scalar=0.0,
                                                       in1=lnb[a % 4][:, lo:512], op0=ALU.max, op1=ALU.add)
                        ve.wait_ge(weighed, NS * hp + a + 1)
                        nc.vector.scalar_tensor_tensor(out=mb[a % 4][:, lo:512], in0=Z[:, lo:512], scalar=0.0,
                                                       in1=lnb[a % 4][:, lo:512], op0=ALU.min,
                                                       op1=ALU.subtract).then_inc(split, 1)
                    if 3 <= i < NS + 3:
                        a = i - 3
                        half, j, u, lo = steps[a]
                        ve.wait_ge(summed, NS * hp + a + 1)
                        nc.vector.tensor_tensor(mb[a % 4][:, lo:512], mb[a % 4][:, lo:512],
                                                [A0, A1][a % 2][:, lo:512], ALU.subtract).then_inc(subbed, 1)
                    if i >= 5 and steps[i - 5][1] == 0 and steps[i - 5][2] == 1:
                        half = steps[i - 5][0]
                        ve.wait_ge(used, NS * hp + i - 5 + 3)
                        nc.vector.tensor_copy(o_sb[:, hp, half * 512:half * 512 + 512],
                                              OB[:, :]).then_inc(out_read, 1)

        @block.gpsimd
        def _(pool):
            pool.sem_inc(added, 4)
            with pool.Fori(0, 4) as hp:
                for i in range(2, NS + 4):
                    if i < NS + 2 and diag[i - 2]:
                        a = i - 2
                        half, j, u, lo = steps[a]
                        pool.wait_ge(split, NS * hp + a + 4)
                        nc.gpsimd.tensor_tensor(L[a % 4][:, lo:lo + P], L[a % 4][:, lo:lo + P],
                                                above[:, :], ALU.mult).then_inc(masked, 1)
                    if 3 <= i < NS + 3:
                        a = i - 3
                        half, j, u, lo = steps[a]
                        pool.wait_ge(summed, NS * hp + a + 1)
                        if a in first_of or a - 1 in first_of:
                            pool.sem_inc(passed, 1)
                            nc.gpsimd.memset(lsum[u][:, 0:lo], 0.0)
                            nc.gpsimd.tensor_copy(lsum[u][:, lo:512], L[a % 4][:, lo:512]).then_inc(added, 1)
                        else:
                            nc.gpsimd.tensor_tensor(lsum[u][:, lo:512], lsum[u][:, lo:512], L[a % 4][:, lo:512],
                                                    ALU.add).then_inc(added, 1)
                    if i >= 4 and diag[i - 4]:
                        a = i - 4
                        half, j, u, lo = steps[a]
                        pool.wait_ge(weighed, NS * hp + a + 5)
                        nc.gpsimd.tensor_tensor(att[a % 2][:, lo:lo + P], att[a % 2][:, lo:lo + P],
                                                above[:, :], ALU.mult).then_inc(cut, 1)

    cks = [at("cks", [P, BW], F32, SCR + 2048 * i) for i in range(3)]
    cvs = [at("cvs", [P, BW], F32, SCR + 6144 + 2048 * i) for i in range(3)]
    ckT = [at("ckT", [P, 4, P], F32, SCR + 12288 + 2048 * i) for i in range(2)]
    NB = PAST // P + 1
    ckd = io["cache_sb_k"].rearrange("l b t h d -> (l b t) (h d)")
    cvd = io["cache_sb_v"].rearrange("l b t h d -> (l b t) (h d)")
    with Stage(nc) as ctx:
        *arrived, turned, copied, scored, logged, split, masked, summed, subbed, weighed, cut, used, added, \
            out_read, evens = sems(ctx, "ss", "arrived0 arrived1 arrived2 turned copied scored logged split masked summed subbed "
                            "weighed cut used added out_read evens")
        block = ctx.enter_context(nc.Block())
        krows = [DEC] + [P] * (NB - 1)
        heads3 = lambda ap, r: ap[0:r, :].rearrange("p (h q) -> p h q", h=SBH)

        @block.sync
        def _(sp):
            for b in range(1, NB):
                if b >= 4:
                    sp.wait_ge(used, b - 2)
                r0 = PAST - b * P
                sp.dma_start(cks[b % 3][:, :], ckd[r0:r0 + P, :]).then_inc(arrived[b % 3], 16)
                sp.dma_start(cvs[b % 3][:, :], cvd[r0:r0 + P, :]).then_inc(arrived[b % 3], 16)

        @block.tensor
        def _(pe):
            for s in range(NB + 2):
                if s < NB:
                    if s >= 1:
                        pe.wait_ge(arrived[s % 3], 32 * ((s - 1) // 3 + 1))
                        if s >= 2:
                            pe.wait_ge(copied, s - 1)
                        for c in range(4):
                            last = nc.tensor.transpose(TB[:, c * P:(c + 1) * P], cks[s % 3][:, c * P:(c + 1) * P],
                                                       ident[:, :])
                        last.then_inc(turned, 1)
                        pe.wait_ge(copied, s)
                    if s >= 2:
                        pe.wait_ge(split, s - 1)
                    r = krows[s]
                    for h in (0, 2, 4, 6, 1, 3, 5, 7):
                        c, hb = h // 2, 64 * (h % 2)
                        if h == 1:
                            last.then_inc(evens, 1)
                            pe.wait_ge(evens, s + 1)
                        kk = ks[hb:hb + 64, c, :] if s == 0 else ckT[s % 2][hb:hb + 64, c, :]
                        last = nc.tensor.matmul([Z0, Z1][s % 2][0:r, h * DEC:(h + 1) * DEC], kk,
                                                qs[hb:hb + 64, c, :], start=True, stop=True)
                    last.then_inc(scored, 1)
                if 1 <= s <= NB:
                    a = s - 1
                    r = krows[a]
                    if a == 0:
                        pe.wait_ge(masked, 1)
                    else:
                        pe.wait_ge(split, a + 1)
                    if a >= 2:
                        pe.wait_ge(subbed, a - 1)
                    A = [A0, A1][a % 2]
                    last = nc.tensor.matmul(A[0:r, :], below[0:r, 0:r], L[a % 3][0:r, :], start=True, stop=(a == 0))
                    if a:
                        pe.wait_ge(added, a + 1)
                        last = nc.tensor.matmul(A[:, :], ones[:, :], lsum[0][:, :], start=False, stop=True)
                    last.then_inc(summed, 1)
                if s >= 2:
                    a = s - 2
                    r = krows[a]
                    if a == 0:
                        pe.wait_ge(cut, 1)
                    else:
                        pe.wait_ge(weighed, a + 1)
                    for h in range(SBH):
                        c, hb = h // 2, 64 * (h % 2)
                        vv = vs if a == 0 else cvs[a % 3]
                        last = nc.tensor.matmul(OB[hb:hb + 64, c * DEC:(c + 1) * DEC], vv[0:r, h * 64:(h + 1) * 64],
                                                att[a % 2][0:r, h * DEC:(h + 1) * DEC], start=(a == 0 and h < 2),
                                                stop=(a == NB - 1), skip_group_check=True)
                    last.then_inc(used, 1)

        @block.scalar
        def _(act):
            nc.scalar.preload_act_table_set("natural_log_exp_and_others")
            for s in range(NB + 1):
                if s < NB:
                    r, b = krows[s], lnb[s % 2]
                    act.wait_ge(scored, s + 1)
                    if s >= 2:
                        act.wait_ge(split, s - 1)
                    nc.scalar.activation(b[0:r, :], [Z0, Z1][s % 2][0:r, :], ACT.Abs)
                    act.drain()
                    nc.scalar.activation(b[0:r, :], b[0:r, :], ACT.Exp, scale=-1.0)
                    act.drain()
                    nc.scalar.activation(b[0:r, :], b[0:r, :], ACT.Ln, bias=1.0).then_inc(logged, 1)
                if s >= 1:
                    a = s - 1
                    act.wait_ge(subbed, a + 1)
                    if a >= 2:
                        act.wait_ge(used, a - 1)
                    nc.scalar.activation(att[a % 2][0:krows[a], :], mb[a % 3][0:krows[a], :], ACT.Exp).then_inc(weighed, 1)

        @block.vector
        def _(ve):
            for s in range(NB + 1):
                if 1 <= s < NB:
                    ve.wait_ge(turned, s)
                    if s >= 3:
                        ve.wait_ge(scored, s - 1)
                    nc.vector.tensor_copy(ckT[s % 2][:, :, :].rearrange("p c k -> p (c k)"), TB[:, :]).then_inc(copied, 1)
                if 1 <= s <= NB:
                    a = s - 1
                    r = krows[a]
                    ve.wait_ge(summed, a + 1)
                    nc.vector.tensor_tensor(mb[a % 3][0:r, :], mb[a % 3][0:r, :], [A0, A1][a % 2][0:r, :],
                                            ALU.subtract).then_inc(subbed, 1)
                if s < NB:
                    r, Z = krows[s], [Z0, Z1][s % 2]
                    ve.wait_ge(logged, s + 1)
                    if s >= 3:
                        ve.wait_ge(added, s - 1)
                        ve.wait_ge(weighed, s - 2)
                    nc.vector.scalar_tensor_tensor(out=L[s % 3][0:r, :], in0=Z[0:r, :], scalar=0.0,
                                                   in1=lnb[s % 2][0:r, :], op0=ALU.max, op1=ALU.add)
                    nc.vector.scalar_tensor_tensor(out=mb[s % 3][0:r, :], in0=Z[0:r, :], scalar=0.0,
                                                   in1=lnb[s % 2][0:r, :], op0=ALU.min, op1=ALU.subtract).then_inc(split, 1)
            ve.wait_ge(used, NB)
            nc.vector.tensor_copy(o_sb[:, :, SEQ:T], OB[:, 0:4 * DEC].rearrange("p (c q) -> p c q", c=4)).then_inc(out_read, 1)

        @block.gpsimd
        def _(pool):
            nc.gpsimd.memset(lsum[0][:, :], 0.0).then_inc(added, 1)
            pool.wait_ge(split, 1)
            mask = above[0:DEC, 0:DEC].unsqueeze(1).to_broadcast([DEC, SBH, DEC])
            nc.gpsimd.tensor_tensor(heads3(L[0], DEC), heads3(L[0], DEC), mask, ALU.mult).then_inc(masked, 1)
            for a in range(NB):
                r = krows[a]
                pool.wait_ge(summed, a + 1)
                if a == 0:
                    pool.drain()
                nc.gpsimd.tensor_tensor(lsum[0][0:r, :], lsum[0][0:r, :], L[a % 3][0:r, :], ALU.add).then_inc(added, 1)
                if a == 0:
                    pool.wait_ge(weighed, 1)
                    nc.gpsimd.tensor_tensor(heads3(att[0], DEC), heads3(att[0], DEC), mask, ALU.mult).then_inc(cut, 1)

    la = at("la", [P, T], F32, OM)
    tt = at("tt", [P, T], F32, OM + TW)
    bs = at("bs", [P, T], F32, OM + 2 * TW)
    keep = at("keep", [P, T], F32, OM + 3 * TW)
    qd = at("qd", [P, T], F32, R3)
    kd = at("kd", [P, T], F32, R3 + TW)
    ke = at("ke", [P, T], F32, R3 + 2 * TW)
    gvT = at("gvT", [P, T], F32, R3 + 3 * TW)
    osq = at("osq", [P, T], F32, R3 + 4 * TW)
    o2 = R3 + 5 * TW
    ken = at("ken", [P, NT, P], F32, o2)
    gvn = at("gvn", [P, NT, P], F32, o2 + 4608)
    atm = at("atm", [P, NT, P], F32, o2 + 9216)
    S = at("S", [P, 19, P], F32, o2 + 13824)
    assert o2 + 13824 + 9728 <= END, o2
    SM = CON + 2560
    NCH = T // CH
    dec = at("dec", [P, NCH], F32, SM)
    gnt = at("gnt", [P, 4], F32, SM + 96)
    bat = at("bat", [P, 2], F32, SM + 128)
    w2c = at("w2c", [RANK, P], F32, SM + 704)
    cmask = at("cmask", [P, P], I32, SM + 192)
    with Stage(nc) as ctx:
        st = Stream(nc, ctx, "g", [3] * 6, wst, whi, wlo)
        consts, small, ranked, w2_ready, shifted, ln_done, scanned, grown, decayed, shrunk, fell, qd_ready, ke_ready, \
            kd_ready, turned, copied, updated, states, paired, kept, outed, squared, moved, summed, logd, rooted, \
            gated, silued, done, stored, passed, st_in0, st_in1 = sems(
                ctx, "gl", "consts small ranked w2_ready shifted ln_done scanned grown decayed shrunk fell qd_ready "
                "ke_ready kd_ready turned copied updated states paired kept outed squared moved summed logd rooted gated "
                "silued done stored passed st_in0 st_in1")
        st_in = [st_in0, st_in1]
        block = ctx.enter_context(nc.Block())
        pb2 = lambda j: [[PA, PB][(3 * j + g) % 2] for g in range(3)]
        gout = io["out4"].rearrange("l b h k v -> (l b h k) v")
        gouts = io["out9"].rearrange("l b h k v -> (l b h k) v")
        gin = io["state_gla"].rearrange("l b h k v -> (l b h k) v")
        cols = lambda j, p: (w_in_k[:, :, bass.ds((C_GQ, C_GK)[j] + p * P, P)] if j < 2 else
                             w_in_k[:, :, bass.ds(((C_GV, C_GR)[j % 2]) + ((j - 2) // 2) * P + p * 2 * P, P)])
        upd = lambda c: ([[Z0, Z1, A0], [A1, OB]][c % 2][c // 8], (c // 2) % 4 * P)
        blk = lambda ap: ap.rearrange("p (c t) -> p c t", t=CH)

        @block.sync
        def _(sp):
            with nc.allow_non_contiguous_dma(reason="a few hundred scalars, once"):
                sp.dma_start(gnt[:, :], io["gla_norm"][0, :].rearrange("(h p) -> p h", p=P)).then_inc(small, 16)
                sp.dma_start(bat[:, :], io["b_gla_a"][0, :].rearrange("(h p) -> p h", p=P)).then_inc(small, 16)

            def state_in(p, u):
                if p:
                    sp.wait_ge(outed, 3 * u + 3)
                sp.dma_start(S[u * 64:u * 64 + 64, 17, :],
                             gin[(2 * p + u) * 64:(2 * p + u + 1) * 64, :]).then_inc(st_in[u], 16)

            def states_out(h):
                u = h % 2
                sp.wait_ge(states, h + 1)
                sp.dma_start(gout[h * 64:h * 64 + 64, :], S[u * 64:u * 64 + 64, 16, :]).then_inc(stored, 16)
                sp.dma_start(gouts[h * 64:h * 64 + 64, :], S[u * 64:u * 64 + 64, 18, :]).then_inc(stored, 16)
            sp.dma_start(w2c[:, :], io["w_gla_a2"][0, :, 0:P]).then_inc(w2_ready, 16)
            for j in range(3):
                st.load(sp, 0, j, cols(j, 0))
            state_in(0, 0)
            state_in(0, 1)
            for j in range(3, 6):
                st.load(sp, 0, j, cols(j, 0))
            sp.wait_ge(ranked, 1)
            sp.dma_start(w2c[:, :], io["w_gla_a2"][0, :, P:2 * P]).then_inc(w2_ready, 16)
            for j in range(3):
                st.load(sp, 1, j, cols(j, 1))
            states_out(0)
            state_in(1, 0)
            st.load(sp, 1, 3, cols(3, 1))
            st.load(sp, 1, 4, cols(4, 1))
            states_out(1)
            state_in(1, 1)
            st.load(sp, 1, 5, cols(5, 1))
            states_out(2)
            states_out(3)
            sp.wait_ge(stored, 32 * 4)

        @block.gpsimd
        def _(pool):
            nc.gpsimd.memset(keep[:, :], 1.0)
            nc.gpsimd.tensor_tensor(osq[:, 0:P], above[:, :], ident[:, :], ALU.add)
            nc.gpsimd.memset(atm[:, :, :], 0.0)
            nc.gpsimd.memset(gvn[:, FULL, :], 0.0)
            nc.gpsimd.memset(S[:, 0, :], 0.0)
            pool.drain()
            nc.gpsimd.memset(blk(keep[:, :])[:, :, 0:1], 0.0)
            nc.gpsimd.memset(osq[0:CH, CH:P], 0.0)
            pool.drain()
            nc.gpsimd.tensor_copy(cmask[:, :], osq[:, 0:P])
            pool.drain()
            pool.sem_inc(consts, 1)

        @block.tensor
        def _(pe):
            def rank(p):
                pe.wait_ge(w2_ready, 16 * p + 16)
                if p:
                    pe.wait_ge(shifted, p)
                for g, (c0, n) in enumerate(WIDE):
                    last = nc.tensor.matmul([Z0, Z1, A0][g][:, 0:n], w2c[:, :], glrT[0:RANK, c0:c0 + n],
                                            start=True, stop=True)
                last.then_inc(ranked, 1)

            def turn(p, q, src):
                for g in range(3):
                    if 9 * p + 3 * q + g:
                        pe.wait_ge(copied, 9 * p + 3 * q + g)
                    for t in range(3 * g, 3 * g + 3):
                        r = rows_of(t)
                        last = nc.tensor.transpose(TB[0:r, (t % 3) * P:(t % 3 + 1) * P],
                                                   src[:, t * P:t * P + r], ident[:, :])
                    last.then_inc(turned, 1)

            def update(h, hb):
                pe.wait_ge(copied, 9 * (h // 2) + 3 * (1 + h % 2) + 3)
                if h == 0:
                    pe.wait_ge(shifted, 2)
                else:
                    pe.wait_ge(logd, h)
                    pe.wait_ge(moved, h)
                for c in range(NCH):
                    b0, t = 64 * (c % 2), c // 2
                    bank, c1 = upd(c)
                    last = nc.tensor.matmul(bank[hb:hb + 64, c1:c1 + P], ken[b0:b0 + 64, t, hb:hb + 64],
                                            gvn[b0:b0 + 64, t, :], start=True, stop=True)
                    if c % 8 == 7 or c == NCH - 1:
                        last.then_inc(updated, 1)

            def attend(p, h, hb):
                pe.wait_ge(states, h + 1)
                pe.wait_ge(kd_ready, p + 1)
                for g, (c0, n) in enumerate(WIDE):
                    for t in range(c0 // P, (c0 + n + P - 1) // P):
                        r = rows_of(t)
                        last = nc.tensor.matmul([Z0, Z1, A0][g][0:r, t * P - c0:t * P - c0 + r],
                                                kd[hb:hb + 64, t * P:t * P + r], qd[hb:hb + 64, t * P:t * P + r],
                                                start=True, stop=True)
                    last.then_inc(paired, 1)
                for g, (c0, n) in enumerate(WIDE):
                    bank = [A1, OB, A0][g]
                    pe.wait_ge(kept, 3 * h + g + 1)
                    for t in range(c0 // P, (c0 + n + P - 1) // P):
                        r = rows_of(t)
                        for c in range(2 * t, 2 * t + r // CH):
                            o = bank[:, c * CH - c0:(c + 1) * CH - c0]
                            nc.tensor.matmul(o, gvn[:, t, :], atm[:, t, (c % 2) * CH:(c % 2) * CH + CH],
                                             start=True, stop=False)
                            last = nc.tensor.matmul(o, S[hb:hb + 64, c if c < 16 else 17, :],
                                                    qd[hb:hb + 64, c * CH:(c + 1) * CH], start=False, stop=True)
                    last.then_inc(outed, 1)

            def squares(h):
                for g, (c0, n) in enumerate(WIDE):
                    pe.wait_ge(squared, 3 * h + g + 1)
                    if g == 2:
                        pe.wait_ge(moved, h + 1)
                    last = nc.tensor.matmul([Z0, Z1, A0][g][:, 0:n], ones[:, :], osq[:, c0:c0 + n],
                                            start=True, stop=True)
                last.then_inc(summed, 1)

            project = lambda p, j: st.project(pe, p, j, xhi, xlo, GROUPS, pb2(j))
            pe.sem_inc(st.product, st.per)
            rank(0)
            for j in range(3):
                project(0, j)
            for p in range(2):
                h = 2 * p
                pe.wait_ge(ke_ready, p + 1)
                turn(p, 0, ke)
                if p == 0:
                    rank(1)
                pe.wait_ge(st.drained, 18 * p + 9 + 2)
                turn(p, 1, gvT)
                update(h, 0)
                project(p, 3)
                attend(p, h, 0)
                project(p, 4)
                squares(h)
                pe.wait_ge(st.drained, 18 * p + 15 + 2)
                turn(p, 2, gvT)
                update(h + 1, 64)
                project(p, 5)
                attend(p, h + 1, 64)
                if p == 0:
                    project(1, 0)
                squares(h + 1)
                if p == 0:
                    project(1, 1)
                    project(1, 2)

        @block.scalar
        def _(act):
            nc.scalar.preload_act_table_set("natural_log_exp_and_others")
            act.sem_inc(st.drained, 2)

            def drain(p, j, dst, scale=1.0):
                for g, (c0, n) in enumerate(GROUPS):
                    st.drain(act, p, j, g)
                    nc.scalar.activation(dst[:, c0:c0 + n], pb2(j)[g][:, 0:n], ACT.Copy,
                                         scale=scale).then_inc(st.drained, 1)

            def softplus(p):
                act.drain()
                act.wait_ge(shifted, p + 1)
                nc.scalar.activation(bs[:, :], la[:, :], ACT.Abs)
                act.drain()
                nc.scalar.activation(bs[:, :], bs[:, :], ACT.Exp, scale=-1.0)
                act.drain()
                nc.scalar.activation(bs[:, :], bs[:, :], ACT.Ln, bias=1.0).then_inc(ln_done, 1)

            def gate(p, h):
                act.drain()
                act.wait_ge(kd_ready, p + 1)
                if h:
                    act.wait_ge(moved, h)
                nc.scalar.activation(tt[:, :], gvT[:, :], ACT.Exp, scale=-1.0).then_inc(gated, 1)

            def square(h):
                if h:
                    act.wait_ge(done, h)
                for g, (c0, n) in enumerate(WIDE):
                    act.wait_ge(outed, 3 * h + g + 1)
                    nc.scalar.activation(osq[:, c0:c0 + n], [A1, OB, A0][g][:, 0:n], ACT.Square).then_inc(squared, 1)

            def root(h):
                act.wait_ge(summed, h + 1)
                for g, (c0, n) in enumerate(WIDE):
                    last = nc.scalar.activation(osq[:, c0:c0 + n], [Z0, Z1, A0][g][:, 0:n], ACT.Ln,
                                                scale=1.0 / P, bias=stat[:, 10:11])
                last.then_inc(logd, 1)
                act.drain()
                nc.scalar.activation(osq[:, :], osq[:, :], ACT.Exp, scale=-0.5).then_inc(rooted, 1)

            for j in range(3):
                st.split_high(act, 0, j)
            softplus(0)
            drain(0, 0, qd, CH ** -0.5)
            for p in range(2):
                h = 2 * p
                act.wait_ge(scanned, p + 1)
                if p:
                    act.wait_ge(moved, h)
                nc.scalar.activation(tt[:, :], bs[:, :], ACT.Exp, scale=1.0 / TAU).then_inc(grown, 1)
                nc.scalar.activation(dec[:, :], blk(bs[:, :])[:, :, CH - 1], ACT.Exp, scale=1.0 / TAU).then_inc(decayed, 1)
                nc.scalar.activation(la[:, :], la[:, :], ACT.Exp, scale=1.0 / TAU).then_inc(fell, 1)
                drain(p, 1, kd)
                st.split_high(act, p, 3)
                st.split_high(act, p, 4)
                act.wait_ge(qd_ready, p + 1)
                nc.scalar.activation(tt[:, :], bs[:, :], ACT.Exp, scale=-1.0 / TAU).then_inc(shrunk, 1)
                drain(p, 2, gvT)
                st.split_high(act, p, 5)
                drain(p, 3, gvT)
                gate(p, h)
                if p == 0:
                    softplus(1)
                square(h)
                if p == 0:
                    st.split_high(act, 1, 0)
                act.wait_ge(silued, h + 1)
                drain(p, 4, gvT)
                root(h)
                if p == 0:
                    st.split_high(act, 1, 1)
                drain(p, 5, gvT)
                gate(p, h + 1)
                square(h + 1)
                if p == 0:
                    st.split_high(act, 1, 2)
                    drain(1, 0, qd, CH ** -0.5)
                root(h + 1)

        @block.vector
        def _(ve):
            nc.vector.memset(stat[:, 10:11], EPS)
            ve.drain()
            ve.sem_inc(st.low, 3)
            ve.wait_ge(small, 32)
            ve.wait_ge(consts, 1)

            def shift(p):
                ve.wait_ge(ranked, p + 1)
                for g, (c0, n) in enumerate(WIDE):
                    last = nc.vector.tensor_scalar(la[:, c0:c0 + n], [Z0, Z1, A0][g][:, 0:n], bat[:, p:p + 1], None, ALU.add)
                last.then_inc(shifted, 1)

            def scan(p):
                ve.wait_ge(ln_done, p + 1)
                nc.vector.scalar_tensor_tensor(out=la[:, :], in0=la[:, :], scalar=0.0, in1=bs[:, :],
                                               op0=ALU.min, op1=ALU.subtract)
                ve.drain()
                nc.vector.tensor_tensor_scan(bs[:, :], keep[:, :], la[:, :], 0.0, ALU.mult, ALU.add)
                ve.drain()
                nc.vector.tensor_tensor(blk(la[:, :]), blk(bs[:, :])[:, :, CH - 1:CH].to_broadcast([P, NCH, CH]),
                                        blk(bs[:, :]), ALU.subtract).then_inc(scanned, 1)

            def copy(p, q, dst):
                for g in range(3):
                    ve.wait_ge(turned, 9 * p + 3 * q + g + 1)
                    full = min(3, FULL - 3 * g)
                    last = nc.vector.tensor_copy(dst[:, 3 * g:3 * g + full, :].rearrange("p a b -> p (a b)"),
                                                 TB[:, 0:full * P])
                    if full < 3:
                        last = nc.vector.tensor_copy(dst[0:DEC, FULL, :], TB[0:DEC, full * P:full * P + P])
                    last.then_inc(copied, 1)

            def advance(p, h, hb):
                ve.wait_ge(st_in[h % 2], 16 * p + 16)
                if h:
                    ve.wait_ge(stored, 32 * h)
                for c in range(NCH):
                    if c % 8 == 0:
                        ve.wait_ge(updated, 3 * h + c // 8 + 1)
                    bank, c1 = upd(c)
                    src, dst = (c, c + 1) if c < 16 else (17, 18)
                    nc.vector.scalar_tensor_tensor(
                        out=S[hb:hb + 64, dst, :], in0=S[hb:hb + 64, src, :], scalar=dec[hb:hb + 64, c:c + 1],
                        in1=bank[hb:hb + 64, c1:c1 + P], op0=ALU.mult, op1=ALU.add)
                    ve.drain()
                ve.sem_inc(states, 1)

            def close(h):
                for g, (c0, n) in enumerate(WIDE):
                    ve.wait_ge(paired, 3 * h + g + 1)
                    ve.sem_inc(passed, 1)
                    t0, nt, r = c0 // P, max(n // P, 1), min(n, P)
                    nc.vector.copy_predicated(
                        atm[0:r, t0:t0 + nt, 0:r], cmask[0:r, 0:r].unsqueeze(1).to_broadcast([r, nt, r]),
                        [Z0, Z1, A0][g][0:r, 0:n].rearrange("p (t q) -> p t q", q=r)).then_inc(kept, 1)
                ve.wait_ge(gated, h + 1)
                nc.vector.tensor_scalar(tt[:, :], tt[:, :], 1.0, None, ALU.add)
                ve.drain()
                nc.vector.reciprocal(tt[:, :], tt[:, :])
                ve.drain()
                nc.vector.tensor_tensor(tt[:, :], tt[:, :], gvT[:, :], ALU.mult).then_inc(silued, 1)
                ve.drain()
                for g, (c0, n) in enumerate(WIDE):
                    ve.wait_ge(squared, 3 * h + g + 1)
                    last = nc.vector.scalar_tensor_tensor(out=o_gla[:, h, c0:c0 + n], in0=[A1, OB, A0][g][:, 0:n],
                                                          scalar=gnt[:, h:h + 1], in1=tt[:, c0:c0 + n],
                                                          op0=ALU.mult, op1=ALU.mult)
                last.then_inc(moved, 1)
                ve.drain()

            def norm(h):
                ve.wait_ge(rooted, h + 1)
                nc.vector.tensor_tensor(o_gla[:, h, :], o_gla[:, h, :], osq[:, :], ALU.mult).then_inc(done, 1)

            for j in range(3):
                st.split_low(ve, 0, j)
            shift(0)
            scan(0)
            for p in range(2):
                h = 2 * p
                ve.wait_ge(grown, p + 1)
                ve.wait_ge(st.drained, 18 * p + 3 + 2)
                nc.vector.tensor_tensor(qd[:, :], qd[:, :], tt[:, :], ALU.mult).then_inc(qd_ready, 1)
                ve.wait_ge(fell, p + 1)
                ve.wait_ge(st.drained, 18 * p + 6 + 2)
                nc.vector.tensor_tensor(ke[:, :], kd[:, :], la[:, :], ALU.mult).then_inc(ke_ready, 1)
                st.split_low(ve, p, 3)
                st.split_low(ve, p, 4)
                ve.wait_ge(shrunk, p + 1)
                nc.vector.tensor_tensor(kd[:, :], kd[:, :], tt[:, :], ALU.mult).then_inc(kd_ready, 1)
                st.split_low(ve, p, 5)
                copy(p, 0, ken)
                if p == 0:
                    shift(1)
                copy(p, 1, gvn)
                ve.wait_ge(decayed, p + 1)
                advance(p, h, 0)
                close(h)
                if p == 0:
                    scan(1)
                    st.split_low(ve, 1, 0)
                norm(h)
                copy(p, 2, gvn)
                advance(p, h + 1, 64)
                if p == 0:
                    st.split_low(ve, 1, 1)
                close(h + 1)
                if p == 0:
                    st.split_low(ve, 1, 2)
                norm(h + 1)

    mhi = at("mhi", [P, KC, NMEM], F32R, R3)
    mlo = at("mlo", [P, KC, NMEM], F32R, R3 + 8192)
    memr = io["mem_prompt"].rearrange("b t d -> (b t) d")
    norm_block("m", [(memr[0:P, :], P, 0), (memr[P:2 * P, :], P, P)], io["norm_mem"][0, :], mhi, mlo, R3 + 16384, False)
    mqT = at("mqT", [P, T], F32, R3 + 16384)
    o4 = R3 + 16384 + TW
    mkT = at("mkT", [P, NMEM], F32, o4)
    mvT = at("mvT", [P, NMEM], F32, o4 + 1024)
    mn = at("mn", [P, 4, P], F32, o4 + 2048)
    cm = at("cm", [P, 4, P], F32, o4 + 4096)
    cmT = at("cmT", [P, NMEM], F32, o4 + 6144)
    pt = [at("pt", [P, 2, NMEM], F32, o4 + 7168 + 2048 * i) for i in range(2)]
    pT = at("pT", [P, 2, T], F32, o4 + 11264)
    assert o4 + 11264 + 2 * TW <= END
    with Stage(nc) as ctx:
        st = Stream(nc, ctx, "mm", [3, 1, 1], wst, whi, wlo)
        cache_in, turned, copied, scored, peaked, expd, scaled, outed, out_read, stored, passed = sems(
            ctx, "me", "cache_in turned copied scored peaked expd scaled outed out_read stored passed")
        block = ctx.enter_context(nc.Block())
        wkv = io["w_mem_kv"][0, :, :].rearrange("(k p) n -> p k n", p=P)
        rows2 = lambda ap, h: ap.rearrange("l b (m p) h d -> p (l b m) (h d)", p=P)[:, :, bass.ds(h * P, P)]
        cols = lambda j, h: (w_in_k[:, :, bass.ds(C_MQ + h * P, P)] if j == 0 else
                             wkv[:, :, bass.ds((j - 1) * BW + h * P, P)])
        mbanks = [[PA, PB, OB], [PA], [PB]]
        QB = [Z0, Z1, A0, A1, Z0]
        VB = [OB, Z1, A0]
        pairs = [(0, 1), (2, 3), (4, 5), (6, 7), (8,)]

        def heads(eng, body):
            with eng.Fori(0, 2) as h:
                body(h, True, True)
            body(2, True, False)
            body(3, False, False)

        @block.sync
        def _(sp):
            for h in range(2):
                for j in range(3):
                    st.load(sp, h, j, cols(j, h))

            def body(h, project, split):
                sp.wait_ge(out_read, 3 * h + 1)
                sp.sem_inc(passed, 1)
                sp.dma_start(cm[:, 0:2, :], rows2(io["cache_mem_k"], h)).then_inc(cache_in, 16)
                sp.dma_start(cm[:, 2:4, :], rows2(io["cache_mem_v"], h)).then_inc(cache_in, 16)
                if split:
                    for j in range(3):
                        st.load(sp, h + 2, j, cols(j, h + 2))
                sp.wait_ge(copied, 7 * h + 3)
                sp.sem_inc(passed, 1)
                sp.dma_start(rows2(io["out5"], h), mn[:, 0:2, :]).then_inc(stored, 16)
                sp.dma_start(rows2(io["out6"], h), mn[:, 2:4, :]).then_inc(stored, 16)
            heads(sp, body)
            sp.wait_ge(stored, 32 * 5)

        @block.tensor
        def _(pe):
            pe.sem_inc(st.product, st.per)
            st.project(pe, 0, 0, xhi, xlo, GROUPS, mbanks[0])
            st.project(pe, 0, 1, mhi, mlo, [(0, NMEM)], mbanks[1])
            st.project(pe, 0, 2, mhi, mlo, [(0, NMEM)], mbanks[2])

            def body(h, project, split):
                def query(g):
                    if project:
                        st.project(pe, h + 1, 0, xhi, xlo, GROUPS, mbanks[0], only=g)

                def score(q):
                    for i, t in enumerate(pairs[q]):
                        r = rows_of(t)
                        last = nc.tensor.matmul(QB[q][0:r, i * NMEM:(i + 1) * NMEM], mqT[:, t * P:t * P + r],
                                                mkT[:, :] if t < FULL else cmT[:, :], start=True, stop=True)
                    last.then_inc(scored, 1)

                def turn(q):
                    pe.wait_ge(scaled, 5 * h + q + 1)
                    pe.wait_ge(copied, 7 * h + 3 + q)
                    pe.sem_inc(passed, 1)
                    for i, t in enumerate(pairs[q]):
                        r = rows_of(t)
                        for m in range(2):
                            last = nc.tensor.transpose(TB[:, (2 * m + i) * P:(2 * m + i) * P + r],
                                                       pt[q % 2][0:r, i, m * P:(m + 1) * P], ident[0:r, 0:r])
                    last.then_inc(turned, 1)

                def weigh(g):
                    c0, n = WIDE[g]
                    pe.wait_ge(copied, 7 * h + [5, 7, 8][g])
                    src = mn if g < 2 else cm
                    for m in range(2):
                        last = nc.tensor.matmul(VB[g][:, 0:n], src[:, 2 + m, :], pT[:, m, c0:c0 + n],
                                                start=(m == 0), stop=(m == 1))
                    last.then_inc(outed, 1)

                pe.wait_ge(st.drained, 5 * h + 5 + 2)
                score(0)
                pe.wait_ge(out_read, 3 * h + 1)
                for q in range(1, 4):
                    score(q)
                pe.wait_ge(cache_in, 32 * h + 32)
                pe.wait_ge(copied, 7 * h + 1)
                for m in range(2):
                    last = nc.tensor.transpose(TB[:, m * P:(m + 1) * P], cm[:, m, :], ident[:, :])
                last.then_inc(turned, 1)
                query(0)
                pe.wait_ge(copied, 7 * h + 2)
                for q, src in enumerate((mkT, mvT)):
                    for m in range(2):
                        last = nc.tensor.transpose(TB[:, (2 * q + m) * P:(2 * q + m + 1) * P],
                                                   src[:, m * P:(m + 1) * P], ident[:, :])
                last.then_inc(turned, 1)
                query(1)
                pe.wait_ge(expd, 5 * h + 1)
                score(4)
                turn(0)
                query(2)
                turn(1)
                if project:
                    st.project(pe, h + 1, 1, mhi, mlo, [(0, NMEM)], mbanks[1])
                turn(2)
                if project:
                    st.project(pe, h + 1, 2, mhi, mlo, [(0, NMEM)], mbanks[2])
                turn(3)
                weigh(0)
                turn(4)
                weigh(1)
                weigh(2)
            heads(pe, body)

        @block.scalar
        def _(act):
            act.sem_inc(st.drained, 2)
            act.sem_inc(out_read, 1)

            def drain(h, j, g):
                dst, scale = ((mqT, P ** -0.5), (mkT, 1.0), (mvT, 1.0))[j]
                c0, n = GROUPS[g] if j == 0 else (0, NMEM)
                st.drain(act, h, j, g)
                nc.scalar.activation(dst[:, c0:c0 + n], mbanks[j][g][:, 0:n], ACT.Copy, scale=scale).then_inc(st.drained, 1)
            for j in range(3):
                st.split_high(act, 0, j)
            for j, g in ((0, 0), (0, 1), (0, 2), (1, 0), (2, 0)):
                drain(0, j, g)
            for j in range(3):
                st.split_high(act, 1, j)

            def body(h, project, split):
                between = {1: ((0, 0), (0, 1)), 2: ((0, 2),), 3: ((1, 0),), 4: ((2, 0),)}
                for q in range(5):
                    act.wait_ge(peaked, 5 * h + q + 1)
                    act.wait_ge(copied, 7 * h + 2 + q)
                    for i, t in enumerate(pairs[q]):
                        r = rows_of(t)
                        last = nc.scalar.activation(pt[q % 2][0:r, i, :], QB[q][0:r, i * NMEM:(i + 1) * NMEM], ACT.Exp,
                                                    bias=nbias[0:r, 2 * q + i:2 * q + i + 1],
                                                    accum_out=stat[0:r, 2 * q + i:2 * q + i + 1])
                    last.then_inc(expd, 1)
                    if project and q in between:
                        for j, g in between[q]:
                            drain(h + 1, j, g)
                for g, (c0, n) in enumerate(WIDE):
                    act.wait_ge(outed, 3 * h + g + 1)
                    nc.scalar.activation(o_mem[:, h, c0:c0 + n], VB[g][:, 0:n], ACT.Copy).then_inc(out_read, 1)
                    if split:
                        st.split_high(act, h + 2, g)
            heads(act, body)

        @block.vector
        def _(ve):
            ve.sem_inc(st.low, 3)
            ve.sem_inc(copied, 1)
            ve.sem_inc(stored, 32)
            for h in range(2):
                for j in range(3):
                    st.split_low(ve, h, j)

            def body(h, project, split):
                def peak(q):
                    r, k = (P, 2) if q < 4 else (DEC, 1)
                    ve.wait_ge(scored, 5 * h + q + 1)
                    nc.vector.tensor_reduce(nbias[0:r, 2 * q:2 * q + k],
                                            QB[q][0:r, 0:k * NMEM].rearrange("p (k m) -> p k m", k=k),
                                            AX.X, ALU.max, negate=True).then_inc(peaked, 1)

                def scale(a):
                    r, k = (P, 2) if a < 4 else (DEC, 1)
                    ve.wait_ge(expd, 5 * h + a + 1)
                    nc.vector.reciprocal(stat[0:r, 16 + 2 * a:16 + 2 * a + k], stat[0:r, 2 * a:2 * a + k])
                    ve.drain()
                    for i in range(k):
                        last = nc.vector.tensor_scalar(pt[a % 2][0:r, i, :], pt[a % 2][0:r, i, :],
                                                       stat[0:r, 16 + 2 * a + i:17 + 2 * a + i], None, ALU.mult)
                    last.then_inc(scaled, 1)

                def turn(q):
                    ve.wait_ge(turned, 7 * h + 3 + q)
                    n = 2 * P if q < 4 else DEC
                    src = TB[:, :].rearrange("p (m c) -> p m c", m=2)[:, :, 0:n]
                    nc.vector.tensor_copy(pT[:, :, 2 * q * P:2 * q * P + n], src).then_inc(copied, 1)
                for q in range(4):
                    peak(q)
                ve.wait_ge(turned, 7 * h + 1)
                nc.vector.tensor_copy(cmT[:, :], TB[:, 0:NMEM]).then_inc(copied, 1)
                scale(0)
                ve.wait_ge(stored, 32 * h + 32)
                ve.wait_ge(turned, 7 * h + 2)
                nc.vector.tensor_copy(mn[:, :, :].rearrange("p a b -> p (a b)"), TB[:, :]).then_inc(copied, 1)
                scale(1)
                peak(4)
                for q in range(5):
                    turn(q)
                    if q < 3:
                        scale(q + 2)
                if split:
                    for j in range(3):
                        st.split_low(ve, h + 2, j)
            heads(ve, body)

    mixT = at("mixT", [P, KC, T], F32, R2)
    o5 = R2 + KC * TW
    wb = [at("wb", [P, 4, P], F32, o5 + 2048 * i) for i in range(3)]
    sg = [at("sg", [P, 384], F32, o5 + 6144 + 1536 * i) for i in range(3)]
    tm = [at("tm", [P, 384], F32, o5 + 6144 + 1536 * (3 + i)) for i in range(2)]
    nil = at("nil", [P, 256], F32, o5 + 6144 + 1536 * 5)
    assert o5 + 6144 + 1536 * 5 + 1024 <= END
    with Stage(nc) as ctx:
        st = Stream(nc, ctx, "e", [3, 3, 3], wst, whi, wlo)
        w0, w1_, w2_, branched, weighed, passed, cleared = sems(ctx, "mx", "w0 w1 w2 branched weighed passed cleared")
        wsem = [w0, w1_, w2_]
        block = ctx.enter_context(nc.Block())
        branch = [o_sb, o_gla, o_mem]
        ebanks = [PA, PB, TB]
        wbr = io["w_branch"][0, :, :, :].rearrange("n (c p) d -> n p c d", p=P)

        @block.sync
        def _(sp):
            with sp.Fori(0, KC) as d:
                for n in range(3):
                    st.load(sp, d, n, w_in_k[:, :, bass.ds(C_GT + n * D + d * P, P)])
                    sp.wait_ge(branched, 9 * d + 3 * n + 3)
                    sp.sem_inc(passed, 1)
                    sp.dma_start(wb[n][:, :, :], wbr[n, :, :, bass.ds(d * P, P)]).then_inc(wsem[n], 16)

        @block.gpsimd
        def _(pool):
            nc.gpsimd.memset(nil[:, :], 0.0)
            pool.drain()
            with pool.Fori(0, OVER) as b:
                dst = ysd[bass.ds(b * P + NE * P, P), :].rearrange("p (a c) -> p a c", c=256)
                pool.dma_start(dst, nil[:, :].unsqueeze(1).to_broadcast([P, D // 256, 256])).then_inc(cleared, 16)
            pool.wait_ge(cleared, 16 * OVER)

        @block.tensor
        def _(pe):
            pe.sem_inc(st.product, st.per)
            pe.sem_inc(branched, 9)
            with pe.Fori(0, KC) as d:
                for n in range(3):
                    st.project(pe, d, n, xhi, xlo, GROUPS, ebanks)
                    pe.wait_ge(wsem[n], 16 * d + 16)
                    for g, (c0, m) in enumerate(GROUPS):
                        pe.wait_ge(weighed, 9 * d + 3 * n + g + 1)
                        for c in range(4):
                            last = nc.tensor.matmul([Z0, Z1, A0][g][:, 0:m], wb[n][:, c, :],
                                                    branch[n][:, c, c0:c0 + m], start=(c == 0), stop=(c == 3))
                        last.then_inc(branched, 1)

        @block.scalar
        def _(act):
            act.sem_inc(st.drained, 3)
            for j in range(3):
                st.split_high(act, 0, j)
            with act.Fori(0, KC) as d:
                for n in range(3):
                    for g, (c0, m) in enumerate(GROUPS):
                        st.drain(act, d, n, g)
                        act.wait_ge(weighed, 9 * d + 3 * n + g + 1)
                        nc.scalar.activation(sg[g][:, 0:m], ebanks[g][:, 0:m], ACT.Sigmoid).then_inc(st.drained, 1)
                    with act.If(d < KC - 1):
                        st.split_high(act, d + 1, n)

        @block.vector
        def _(ve):
            ve.sem_inc(st.low, 3)
            ve.sem_inc(weighed, 3)
            for j in range(3):
                st.split_low(ve, 0, j)
            with ve.Fori(0, KC) as d:
                for n in range(3):
                    for g, (c0, m) in enumerate(GROUPS):
                        ve.wait_ge(st.drained, 9 * d + 3 * n + g + 4)
                        ve.wait_ge(branched, 9 * d + 3 * n + g + 10)
                        b = [Z0, Z1, A0][g][:, 0:m]
                        if n == 0:
                            nc.vector.tensor_tensor(mixT[:, d, c0:c0 + m], sg[g][:, 0:m], b, ALU.mult).then_inc(weighed, 1)
                        else:
                            nc.vector.tensor_tensor(tm[(3 * n + g) % 2][:, 0:m], sg[g][:, 0:m], b, ALU.mult).then_inc(weighed, 1)
                            ve.drain()
                            nc.vector.tensor_tensor(mixT[:, d, c0:c0 + m], mixT[:, d, c0:c0 + m],
                                                    tm[(3 * n + g) % 2][:, 0:m], ALU.add)
                    with ve.If(d < KC - 1):
                        st.split_low(ve, d + 1, n)

    wgd = io["w_e_gate"][0, :, :, :].rearrange("e (p k) n -> e p k n", p=P)
    wud = io["w_e_up"][0, :, :, :].rearrange("e (p k) n -> e p k n", p=P)
    wdd = io["w_e_down"][0, :, :, :].rearrange("e (p k) n -> e p k n", p=P)
    wo_s = at("wo_s", [P, KC, D], F32, 0)
    wo_h = at("wo_h", [P, KC, D], F32R, 32768)
    wo_l = at("wo_l", [P, KC, D], F32R, 65536)
    f = 98304
    tile_h = [at("tile_h", [P, KC, P], F32R, f + 4096 * i) for i in range(2)]
    tile_l = [at("tile_l", [P, KC, P], F32R, f + 8192 + 4096 * i) for i in range(2)]
    xt = [at("xt", [P, D], F32, f + 16384 + 4096 * i) for i in range(2)]
    hlast = at("hlast", [P, KC, P], F32, f + 45056)
    hrow = lambda n, rows: (hlast[0:rows, :, :] if isinstance(n, int) and n == FULL else mixT[0:rows, :, bass.ds(n * P, P)])
    wide = lambda ap: ap.rearrange("p (k c) -> p k c", c=P)
    nrow = [at("nrow", [P, D], F32, f + 32768 + 4096 * i) for i in range(2)]
    nT = at("nT", [P, KC, P], F32, f + 40960)
    gb = at("gb", [P, D], F32, f + 24576)
    wr = at("wr", [P, KC, NG + NE], F32, f + 49152)
    f = f + 49152 + 1152
    br = at("br", [P, NG + NE], F32, f)
    lgc = at("lgc", [P, 8], F32, f + 160)
    lgf = at("lgf", [P, NE], F32, f + 192)
    top8 = at("top8", [P, 16], F32, f + 320)
    idx8 = at("idx8", [P, 16], U32, f + 384)
    idf = at("idf", [P, 8], F32, f + 448)
    oh4 = at("oh4", [P, NG], F32, f + 480)
    gsel = at("gsel", [P, NG, EPG], F32, f + 512)
    sel = at("sel", [P, EPG], F32, f + 640)
    sc = at("sc", [P, 8], F32, f + 672)
    ohs = at("ohs", [P, NE], F32, f + 704)
    oht = at("oht", [P, NE], F32, f + 832)
    f = f + 960
    oh = at("oh", [P, 2, NT, NE], F32, f)
    rank = at("rank", [P, NT, NE], F32, f + 2304)
    iot = at("iot", [P, NE], F32, f + 3456)
    ioti = at("ioti", [P, NE], I32, f + 3584)
    thr = at("thr", [P, OVER], F32, f + 3712)
    f = f + 3712 + 64 * ((OVER * 4 + 63) // 64)
    thri = at("thri", [P, OVER], I32, f)
    f = f + 64 * ((OVER * 4 + 63) // 64)
    cnt = at("cnt", [P, NE], F32, f)
    nov = at("nov", [P, NE], F32, f + 128)
    pre = at("pre", [P, NE], F32, f + 256)
    inc = at("inc", [P, NE], F32, f + 384)
    zero32 = at("zero32", [P, NE], F32, f + 512)
    base1 = at("base1", [P, NE], F32, f + 640)
    f = f + 768
    zfill = at("zfill", [P, SLOTS // P + 2], I32, f)
    tok = at("tok", [P, NT], I32, f + 384)
    mslot = at("mslot", [P, NE], F32, f + 448)
    mprod = at("mprod", [P, 2, NE], F32, f + 576)
    midf = at("midf", [P, 2], F32, f + 832)
    midx = at("midx", [P, NT, 2], I32, f + 864)
    scur = at("scur", [P, 3], I32, f + 960)
    nobody = at("nobody", [P, 2], F32, f + 992)
    f = f + 1024
    assert f <= R2 - 4096, f
    f = R2 + KC * TW
    sq = at("sq", [P, D], F32, f)
    slot = at("slot", [P, NT, NE], F32, f + 4096)
    isov = at("isov", [P, NT, NE], F32, f + 5248)
    prod = at("prod", [P, NT, NE], F32, f + 6400)
    cmp = at("cmp", [P, NE * OVER], F32, f + 7552)
    assert f + 7552 + 4 * NE * OVER <= END
    wg = [at("wg", [P, KC, DE], F32, 49152 * i) for i in range(2)]
    wu = [at("wu", [P, KC, DE], F32, 49152 * i + 16384) for i in range(2)]
    wd = [at("wd", [P, 4, D], F32, 49152 * i + 32768) for i in range(2)]
    K0 = SM
    wts = at("wts", [P, NT, 2], F32, K0)
    sidx = [at("sidx", [P, NT], I32, K0 + 96 + 64 * k) for k in range(2)]
    sflt = [at("sflt", [P, NT], F32, K0 + 224 + 64 * k) for k in range(2)]
    ovi = at("ovi", [P, OVER + 1], I32, K0 + 352)
    ovf = at("ovf", [P, OVER + 1], F32, K0 + 512)
    with Stage(nc) as ctx:
        *w_in_s, gains, split_h, split_l, x0, x1, mhigh, mlow, hdone, sq_done, inverted, rooted, ndone, mixed, turned, ncopied, \
            logged, early, argued, expd, picked, ranked, taken, stored, consts, filled, scat, counted, found, ready, saved, \
            placed, again = sems(
                ctx, "f", "w_in0 w_in1 w_in2 w_in3 gains split_h split_l x0 x1 mhigh mlow hdone sq_done inverted rooted ndone mixed turned "
                "ncopied logged early argued expd picked ranked taken stored consts filled scat counted found ready saved placed again")
        xsem = [x0, x1]
        block = ctx.enter_context(nc.Block())

        def each(eng, body):
            with eng.Fori(0, FULL // 2) as i:
                for u in range(2):
                    body(i * 2 + u, i, u, P)
            body(FULL, FULL // 2, 0, DEC)

        def skewed(eng, *parts):
            def step(i):
                for lag, part in parts:
                    if 0 <= i - lag <= FULL:
                        part(i - lag, (i - lag) // 2, (i - lag) % 2, rows_of(i - lag))
            for i in range(-1, 3):
                step(i)
            with eng.Fori(0, 2) as r:
                for i in range(3, 5):
                    for lag, part in parts:
                        part(r * 2 + (i - lag), r + (i - lag) // 2, (i - lag) % 2, P)
            for i in range(7, FULL + 4):
                step(i)

        @block.sync
        def _(sp):
            for q in range(4):
                sp.dma_start(wo_s[:, 2 * q:2 * q + 2, :],
                             io["w_out"][0, 256 * q:256 * q + 256, :].rearrange("(k p) n -> p k n", p=P)).then_inc(w_in_s[q], 16)
            with nc.allow_non_contiguous_dma(reason="router weights, once"):
                sp.dma_start(wr[:, :, 0:NG], io["w_coarse"][0, :, :].rearrange("(k p) e -> p k e", p=P)).then_inc(gains, 16)
                for g in range(NG):
                    sp.dma_start(wr[:, :, NG + g * EPG:NG + (g + 1) * EPG],
                                 io["w_fine"][0, g, :, :].rearrange("(k p) e -> p k e", p=P)).then_inc(gains, 16)
            sp.dma_start(gb[:, :], io["norm_ffn"][0, :].partition_broadcast(P)).then_inc(gains, 16)
            sp.dma_start(br[:, 0:NG], io["b_coarse"][0, :].partition_broadcast(P)).then_inc(gains, 16)
            sp.dma_start(br[:, NG:NG + NE], io["b_fine"][0, :, :].rearrange("g e -> (g e)").partition_broadcast(P)).then_inc(gains, 16)

            def body(n, turn, u, rows):
                sp.wait_ge(hdone, n + 1)
                sp.sem_inc(ready, 1)
                src = xs[:, :] if isinstance(n, int) else xp[bass.ds(n * P, P), :]
                sp.dma_start(xt[u][0:rows, :], src).then_inc(xsem[u], 16)
            each(sp, body)
            sp.wait_ge(split_l, KC)
            sp.dma_start(wg[0][:, :, :], wgd[0, :, :, :]).then_inc(early, 16)
            sp.dma_start(wu[0][:, :, :], wud[0, :, :, :]).then_inc(early, 16)
            sp.wait_ge(mixed, NT + 2)
            sp.dma_start(wd[0][:, :, :], wdd[0, :, :, :]).then_inc(early, 16)
            sp.dma_start(wg[1][:, :, :], wgd[1, :, :, :]).then_inc(early, 16)
            sp.dma_start(wu[1][:, :, :], wud[1, :, :, :]).then_inc(early, 16)
            sp.dma_start(wd[1][:, :, :], wdd[1, :, :, :]).then_inc(early, 16)
            sp.wait_ge(early, 16 * 6)

        @block.gpsimd
        def _(pool):
            nc.gpsimd.iota(ioti[:, :], [[1, NE]], base=0, channel_multiplier=0)
            nc.gpsimd.iota(thri[:, :], [[1, OVER]], base=0, channel_multiplier=0)
            nc.gpsimd.iota(tok[:, :], [[P, NT]], base=0, channel_multiplier=1)
            nc.gpsimd.memset(zfill[:, :], 0)
            nc.gpsimd.memset(oh[:, :, :, :], 0.0)
            nc.gpsimd.memset(rank[:, FULL, :], 0.0)
            nc.gpsimd.memset(ohs[:, :], 0.0)
            nc.gpsimd.memset(zero32[:, :], 0.0)
            nc.gpsimd.memset(lgc[:, :], -3e38)
            pool.drain()
            pool.sem_inc(consts, 1)
            pool.dma_start(slot_tok.rearrange("(p a) one -> p (a one)", p=P), zfill[:, :]).then_inc(filled, 16)
            pool.wait_ge(filled, 16)

            def body(n, turn, u, rows):
                pool.wait_ge(ndone, n + 1)
                pool.sem_inc(ready, 1)
                pool.dma_start(htd[bass.ds(n * P, rows), :], nrow[u][0:rows, :]).then_inc(stored, 16)
                pool.wait_ge(stored, 16 * n + 16)
                pool.sem_inc(saved, 1)
            pool.sem_inc(saved, 2)

            def scatter(n, turn, u, rows):
                pool.wait_ge(placed, n + 1)
                pool.sem_inc(ready, 1)
                nc.gpsimd.tensor_copy(scur[0:rows, 0:2], midx[0:rows, n, :])
                nc.gpsimd.tensor_copy(scur[0:rows, 2:3], tok[0:rows, bass.ds(n, 1)])
                pool.drain()
                for k in range(2):
                    pool.indirect_dma_start(slot_tok, bass.IndirectOffsetOnAxis(ap=scur[0:rows, k:k + 1], axis=0),
                                            scur[0:rows, 2:3], None).then_inc(scat, 16)
                pool.wait_ge(scat, 32 * n + 32)
                pool.sem_inc(ready, 1)
            skewed(pool, (0, body), (3, scatter))
            pool.wait_ge(found, 1)
            many = pool.value_load(ovi[0:1, OVER:OVER + 1], min_val=0, max_val=OVER)
            with pool.If(many > 0):
                for k in range(2):
                    for t in range(NT):
                        r = rows_of(t)
                        pool.indirect_dma_start(slot_tok, bass.IndirectOffsetOnAxis(ap=sidx[k][0:r, t:t + 1], axis=0),
                                                tok[0:r, t:t + 1], None).then_inc(again, 16)
                pool.wait_ge(again, 16 * 2 * NT)

        @block.tensor
        def _(pe):
            pe.sem_inc(mixed, 2)
            pe.wait_ge(consts, 1)
            pe.wait_ge(split_l, KC)
            pe.wait_ge(gains, 16 * 8)

            def project(n, turn, u, rows):
                pe.wait_ge(mlow, n + 1)
                pe.wait_ge(hdone, n + 1)
                for half in range(2):
                    three = [(tile_h[u][:, k, 0:rows], tile_l[u][:, k, 0:rows],
                              wo_h[:, k, half * 512:half * 512 + 512], wo_l[:, k, half * 512:half * 512 + 512])
                             for k in range(KC)]
                    last = three_pass(nc, [[Z0, Z1], [PA, PB]][u][half][0:rows, :], three)
                last.then_inc(mixed, 1)

            def route(n, turn, u, rows):
                pe.wait_ge(ndone, n + 1)
                for q in range(2):
                    pe.wait_ge(ncopied, 2 * n + q + 1)
                    for k in range(4):
                        kk = 4 * q + k
                        last = nc.tensor.transpose([A0, A1][q][:, k * P:k * P + rows],
                                                   nrow[u][0:rows, kk * P:(kk + 1) * P], ident[0:rows, 0:rows])
                    last.then_inc(turned, 1)
                pe.wait_ge(ncopied, 2 * n + 4)
                pe.wait_ge(argued, n + 1)
                for k in range(KC):
                    last = nc.tensor.matmul(OB[0:rows, 0:NG + NE], nT[:, k, 0:rows], wr[:, k, :],
                                            start=(k == 0), stop=(k == KC - 1))
                last.then_inc(logged, 1)

            def count(n, turn, u, rows):
                pe.wait_ge(picked, n + 1)
                pe.wait_ge(taken, n + 1)
                nc.tensor.matmul(TB[0:rows, 0:NE], above[0:rows, 0:rows], oht[0:rows, :], start=True, stop=False)
                nc.tensor.matmul(TB[0:rows, 0:NE], ones[:, 0:rows], ohs[:, :], start=False, stop=True).then_inc(ranked, 1)
            skewed(pe, (0, project), (1, route), (2, count))
            pe.wait_ge(taken, NT + 1)
            nc.tensor.matmul(TB[:, 0:NE], ones[:, :], ohs[:, :], start=True, stop=True).then_inc(counted, 1)

        @block.scalar
        def _(act):
            for k in range(KC):
                if k % 2 == 0:
                    act.wait_ge(w_in_s[k // 2], 16)
                nc.scalar.activation(wo_h[:, k, :], wo_s[:, k, :], ACT.Copy).then_inc(split_h, 1)

            def high(n, turn, u, rows):
                act.wait_ge(mixed, n + 1)
                nc.scalar.activation(tile_h[u][:, :, 0:rows], mixT[:, :, bass.ds(n * P, rows)], ACT.Copy).then_inc(mhigh, 1)

            def norm(n, turn, u, rows):
                act.wait_ge(hdone, n + 3)
                act.sem_inc(ready, 1)
                nc.scalar.activation(wide(sq[0:rows, :]), hrow(n, rows), ACT.Square,
                                     scale=D ** -0.5, accum_out=stat[0:rows, 0:1]).then_inc(sq_done, 1)
                act.wait_ge(inverted, n + 1)
                nc.scalar.activation(stat[0:rows, 2:3], stat[0:rows, 1:2], ACT.Sqrt).then_inc(rooted, 1)

            def copy(n, turn, u, rows):
                for q in range(2):
                    act.wait_ge(turned, 2 * n + q + 1)
                    nc.scalar.activation(nT[:, 4 * q:4 * q + 4, 0:rows],
                                         [A0, A1][q][:, :].rearrange("p (k t) -> p k t", k=4)[:, :, 0:rows],
                                         ACT.Copy).then_inc(ncopied, 1)

            def exps(n, turn, u, rows):
                act.wait_ge(argued, n + 2)
                nc.scalar.activation(sc[0:rows, 4:8], lgc[0:rows, 0:4], ACT.Exp, bias=sc[0:rows, 0:1],
                                     accum_out=sc[0:rows, 1:2])
                nc.scalar.activation(stat[0:rows, 4:5], stat[0:rows, 3:4], ACT.Exp).then_inc(expd, 1)
            act.sem_inc(ncopied, 2)
            skewed(act, (2, exps), (-1, high), (1, copy), (0, norm))

        @block.vector
        def _(ve):
            ve.sem_inc(hdone, 2)
            ve.sem_inc(argued, 1)
            ve.sem_inc(taken, 1)
            for k in range(KC):
                ve.wait_ge(split_h, k + 1)
                nc.vector.tensor_tensor(wo_l[:, k, :], wo_s[:, k, :], wo_h[:, k, :].bitcast(F32), ALU.subtract).then_inc(split_l, 1)
            ve.wait_ge(gains, 16 * 8)
            ve.wait_ge(consts, 1)
            nc.vector.tensor_copy(iot[:, :], ioti[:, :])
            nc.vector.tensor_copy(thr[:, :], thri[:, :])
            ve.drain()
            nc.vector.tensor_scalar(base1[:, :], iot[:, :], float(P), None, ALU.mult)
            nc.vector.tensor_copy(nobody[:, 0:1], tok[:, 0:1])
            nc.vector.tensor_copy(nobody[:, 1:2], tok[:, 1:2])
            ve.drain()
            nc.vector.tensor_scalar(nobody[:, :], nobody[:, :], float(SLOTS), None, ALU.add)
            ve.drain()

            def low(n, turn, u, rows):
                ve.wait_ge(mhigh, n + 1)
                nc.vector.tensor_tensor(tile_l[u][:, :, 0:rows], mixT[:, :, bass.ds(n * P, rows)],
                                        tile_h[u][:, :, 0:rows].bitcast(F32), ALU.subtract).then_inc(mlow, 1)

            def residual(n, turn, u, rows):
                R = slice(0, rows)
                ve.wait_ge(xsem[u], turn * 16 + 16)
                ve.wait_ge(saved, n + 1)
                ve.wait_ge(mixed, n + 3)
                for half in range(2):
                    c = slice(half * 512, half * 512 + 512)
                    last = nc.vector.tensor_tensor(hrow(n, rows)[:, 4 * half:4 * half + 4, :], wide(xt[u][R, c]),
                                                   wide([[Z0, Z1], [PA, PB]][u][half][R, :]), ALU.add)
                last.then_inc(hdone, 1)
                ve.wait_ge(sq_done, n + 1)
                nc.vector.tensor_scalar(stat[R, 1:2], stat[R, 0:1], EPS, None, ALU.add)
                ve.drain()
                nc.vector.reciprocal(stat[R, 1:2], stat[R, 1:2]).then_inc(inverted, 1)
                ve.wait_ge(rooted, n + 1)
                nc.vector.scalar_tensor_tensor(out=wide(nrow[u][R, :]), in0=hrow(n, rows), scalar=stat[R, 2:3], in1=wide(gb[R, :]),
                                               op0=ALU.mult, op1=ALU.mult).then_inc(ndone, 1)

            def choose(n, turn, u, rows):
                R = slice(0, rows)
                ve.wait_ge(logged, n + 1)
                nc.vector.tensor_tensor(lgc[R, 0:NG], OB[R, 0:NG], br[R, 0:NG], ALU.add)
                nc.vector.tensor_tensor(lgf[R, :], OB[R, NG:NG + NE], br[R, NG:], ALU.add)
                ve.drain()
                nc.vector.max(top8[R, 0:8], lgc[R, :])
                ve.drain()
                nc.vector.max_index(idx8[R, 0:8], top8[R, 0:8], lgc[R, :])
                nc.vector.tensor_scalar(sc[R, 0:1], top8[R, 0:1], -1.0, None, ALU.mult)
                ve.drain()
                nc.vector.tensor_copy(idf[R, 0:1], idx8[R, 0:1])
                ve.drain()
                nc.vector.tensor_scalar(oh4[R, :], iot[R, 0:NG], idf[R, 0:1], None, ALU.is_equal)
                ve.drain()
                nc.vector.tensor_tensor(gsel[R, :, :], lgf[R, :].rearrange("p (g e) -> p g e", g=NG),
                                        oh4[R, :].unsqueeze(2).to_broadcast([rows, NG, EPG]), ALU.mult)
                ve.drain()
                nc.vector.tensor_reduce(sel[R, :], gsel[R, :, :].rearrange("p g e -> p e g"), AX.X, ALU.add)
                ve.drain()
                nc.vector.max(top8[R, 8:16], sel[R, :])
                ve.drain()
                nc.vector.max_index(idx8[R, 8:16], top8[R, 8:16], sel[R, :])
                nc.vector.tensor_tensor(stat[R, 3:4], top8[R, 9:10], top8[R, 8:9], ALU.subtract)
                ve.drain()
                ve.sem_inc(argued, 1)
                nc.vector.tensor_copy(idf[R, 2:4], idx8[R, 8:10])
                ve.drain()
                for k in range(2):
                    nc.vector.scalar_tensor_tensor(out=idf[R, 4 + k:5 + k], in0=idf[R, 0:1], scalar=float(EPG),
                                                   in1=idf[R, 2 + k:3 + k], op0=ALU.mult, op1=ALU.add)
                ve.drain()
                for k in range(2):
                    nc.vector.tensor_scalar(oh[R, k, n, :], iot[R, :], idf[R, 4 + k:5 + k], None, ALU.is_equal)
                ve.drain()
                nc.vector.tensor_tensor(oht[R, :], oh[R, 0, n, :], oh[R, 1, n, :], ALU.add).then_inc(picked, 1)
                ve.wait_ge(expd, n + 1)
                nc.vector.tensor_scalar(sc[R, 2:3], stat[R, 4:5], 1.0, None, ALU.add)
                ve.drain()
                nc.vector.tensor_tensor(sc[R, 2:3], sc[R, 2:3], sc[R, 1:2], ALU.mult)
                ve.drain()
                nc.vector.reciprocal(wts[R, n, 0:1], sc[R, 2:3])
                ve.drain()
                nc.vector.tensor_tensor(wts[R, n, 1:2], wts[R, n, 0:1], stat[R, 4:5], ALU.mult)
                ve.drain()

            def take(n, turn, u, rows):
                R = slice(0, rows)
                ve.wait_ge(ranked, n + 1)
                nc.vector.tensor_copy(rank[R, n, :], TB[R, 0:NE])
                nc.vector.tensor_tensor(ohs[R, :], ohs[R, :], oht[R, :], ALU.add)
                ve.drain()
                ve.sem_inc(taken, 1)
                nc.vector.tensor_scalar(mslot[R, :], rank[R, n, :], float(MAIN), float(2 * SLOTS), ALU.is_ge, ALU.mult)
                ve.drain()
                nc.vector.tensor_tensor(mslot[R, :], mslot[R, :], rank[R, n, :], ALU.add)
                ve.drain()
                nc.vector.tensor_tensor(mslot[R, :], mslot[R, :], base1[R, :], ALU.add)
                ve.drain()
                for k in range(2):
                    nc.vector.tensor_tensor(mprod[R, k, :], mslot[R, :], oh[R, k, n, :], ALU.mult)
                ve.drain()
                nc.vector.tensor_reduce(midf[R, :], mprod[R, :, :], AX.X, ALU.add)
                ve.drain()
                nc.vector.tensor_tensor(midf[R, :], midf[R, :], nobody[R, :], ALU.min)
                ve.drain()
                nc.vector.tensor_copy(midx[R, n, :], midf[R, :]).then_inc(placed, 1)
                ve.drain()
            skewed(ve, (3, take), (2, choose), (-1, low), (0, residual))

            ve.wait_ge(counted, 1)
            nc.vector.tensor_copy(cnt[:, :], TB[:, 0:NE])
            nc.vector.tensor_scalar(thr[:, :], thr[:, :], float(P), float(MAIN), ALU.mult, ALU.add)
            ve.drain()
            c3 = cmp[:, :].rearrange("p (e b) -> p e b", e=NE)
            nc.vector.tensor_tensor(c3, cnt[:, :].unsqueeze(2).to_broadcast([P, NE, OVER]),
                                    thr[:, :].unsqueeze(1).to_broadcast([P, NE, OVER]), ALU.is_gt)
            ve.drain()
            nc.vector.tensor_reduce(nov[:, :], c3, AX.X, ALU.add)
            ve.drain()
            nc.vector.tensor_tensor_scan(inc[:, :], nov[:, :], zero32[:, :], 0.0, ALU.add, ALU.add)
            ve.drain()
            nc.vector.tensor_tensor(pre[:, :], inc[:, :], nov[:, :], ALU.subtract)
            c4 = cmp[:, :].rearrange("p (b e) -> p b e", e=NE)
            nc.vector.tensor_scalar(thr[:, :], thr[:, :], float(-MAIN), 1.0 / P, ALU.add, ALU.mult)
            ve.drain()
            nc.vector.tensor_tensor(c4, inc[:, :].unsqueeze(1).to_broadcast([P, OVER, NE]),
                                    thr[:, :].unsqueeze(2).to_broadcast([P, OVER, NE]), ALU.is_le)
            ve.drain()
            nc.vector.tensor_reduce(ovf[:, 0:OVER], c4, AX.X, ALU.add)
            nc.vector.tensor_copy(ovf[:, OVER:OVER + 1], inc[:, NE - 1:NE])
            nc.vector.tensor_scalar(pre[:, :], pre[:, :], float(P), float(NE * P - MAIN), ALU.mult, ALU.add)
            ve.drain()
            nc.vector.tensor_scalar(ovf[:, 0:OVER], ovf[:, 0:OVER], float(NE - 1), None, ALU.min)
            nc.vector.tensor_tensor(pre[:, :], pre[:, :], base1[:, :], ALU.subtract)
            nc.vector.tensor_scalar(isov[:, :, :], rank[:, :, :], float(MAIN), None, ALU.is_ge)
            nc.vector.tensor_tensor(slot[:, :, :], rank[:, :, :], base1[:, :].unsqueeze(1).to_broadcast([P, NT, NE]), ALU.add)
            ve.drain()
            nc.vector.tensor_copy(ovi[:, :], ovf[:, :])
            nc.vector.tensor_tensor(isov[:, :, :], isov[:, :, :], pre[:, :].unsqueeze(1).to_broadcast([P, NT, NE]), ALU.mult)
            ve.drain()
            nc.vector.tensor_tensor(slot[:, :, :], slot[:, :, :], isov[:, :, :], ALU.add)
            ve.drain()
            for k in range(2):
                nc.vector.tensor_tensor(prod[:, :, :], slot[:, :, :], oh[:, k, :, :], ALU.mult)
                ve.drain()
                nc.vector.tensor_reduce(sflt[k][:, :], prod[:, :, :], AX.X, ALU.add)
                ve.drain()
                nc.vector.tensor_copy(sidx[k][:, :], sflt[k][:, :])
                ve.drain()
            ve.sem_inc(found, 1)

    e0 = 98304
    xe = [at("xe", [P, D], F32, e0 + 4096 * i) for i in range(2)]
    xeT = [at("xeT", [P, KC, P], F32, e0 + 8192 + 4096 * i) for i in range(2)]
    gl = [at("gl", [P, DE], F32, e0 + 16384 + 2048 * i) for i in range(2)]
    hT = [at("hT", [P, 4, P], F32, e0 + 20480 + 2048 * i) for i in range(2)]
    ye = [at("ye", [P, D], F32, e0 + 24576 + 4096 * i) for i in range(2)]
    toks = at("toks", [P, NE + OVER], I32, e0 + 32768)
    tcur = [at("tcur", [P, 1], I32, e0 + 33792 + 32 * i) for i in range(2)]
    NB = NE + OVER
    trows = at("trows", [NB, P], I32, e0 + 34304)
    tflt = at("tflt", [NB, P], F32, e0 + 34816)
    with Stage(nc) as ctx:
        toks_in, named, f0, f1, g0, g1, u0, u1, d0, d1, turned, copied, hidden, silued, multiplied, hturned, hcopied, downed, \
            read, s0, s1, passed = sems(ctx, "x", "toks_in named f0 f1 g0 g1 u0 u1 d0 d1 turned copied hidden silued multiplied "
                                        "hturned hcopied downed read s0 s1 passed")
        fetched, gin_, uin_, din_, stored = [f0, f1], [g0, g1], [u0, u1], [d0, d1], [s0, s1]
        block = ctx.enter_context(nc.Block())

        def further(eng, body):
            many = eng.value_load(ovi[0:1, OVER:OVER + 1], min_val=0, max_val=OVER)
            with eng.If(many > 0):
                with eng.Fori(0, OVER // 2) as i:
                    for u in range(2):
                        with eng.If(many > i * 2 + u):
                            e = None
                            if eng.engine == nc.sync.engine:
                                e = eng.value_load(ovi[0:1, bass.ds(i * 2 + u, 1)], min_val=0, max_val=NE - 1)
                            body(NE + i * 2 + u, NE // 2 + i, u, e)

        def each(eng, body):
            with eng.Fori(0, NE // 2) as i:
                for u in range(2):
                    body(i * 2 + u, i, u, i * 2 + u)
            further(eng, body)

        def piped(eng, head, step, tail):
            head(0, 0, 0)
            with eng.Fori(0, NE // 2 - 1) as i:
                step(i * 2 + 1, i, 1)
                step(i * 2 + 2, i + 1, 0)
            step(NE - 1, NE // 2 - 1, 1)
            tail(NE - 1, NE // 2 - 1, 1)
        prev = lambda n, turn, u: (n - 1, turn - 1 + u, 1 - u)
        succ = lambda n, turn, u: (n + 1, turn + u, 1 - u)

        @block.sync
        def _(sp):
            sp.dma_start(trows[:, :], slot_tok[0:SLOTS, :].rearrange("(b p) one -> b (p one)", p=P)).then_inc(toks_in, 16)

            def body(n, turn, u, e):
                sp.wait_ge(hidden, 2 * n + 1)
                sp.sem_inc(passed, 1)
                sp.dma_start(wg[u][:, :, :], wgd[bass.ds(e, 1), :, :, :].rearrange("e p k n -> (e p) k n")).then_inc(gin_[u], 16)
                sp.wait_ge(hidden, 2 * n + 2)
                sp.sem_inc(passed, 1)
                sp.dma_start(wu[u][:, :, :], wud[bass.ds(e, 1), :, :, :].rearrange("e p k n -> (e p) k n")).then_inc(uin_[u], 16)
                sp.wait_ge(downed, n + 1)
                sp.sem_inc(passed, 1)
                sp.dma_start(wd[u][:, :, :], wdd[bass.ds(e, 1), :, :, :].rearrange("e p k n -> (e p) k n")).then_inc(din_[u], 16)
            for arrived in gin_ + uin_ + din_:
                sp.sem_inc(arrived, 16)
            with sp.Fori(1, NE // 2) as i:
                for u in range(2):
                    body(i * 2 + u, i, u, i * 2 + u)
            further(sp, body)

        @block.gpsimd
        def _(pool):
            pool.wait_ge(named, 2)

            def body(n, turn, u, e):
                pool.wait_ge(copied, 2 * n + 2)
                nc.gpsimd.tensor_copy(tcur[u][:, :], toks[:, bass.ds(n, 1)])
                pool.drain()
                pool.indirect_dma_start(xe[u][:, :], None, htd,
                                        bass.IndirectOffsetOnAxis(ap=tcur[u][:, :], axis=0)).then_inc(fetched[u], 16)
            each(pool, body)

        @block.tensor
        def _(pe):
            pe.sem_inc(downed, 2)
            pe.sem_inc(hidden, 4)
            pe.wait_ge(named, 1)
            nc.tensor.transpose(TB[:, 0:NB], tflt[:, :], ident[0:NB, 0:NB]).then_inc(hturned, 1)

            def turn_x(n, turn, u):
                pe.wait_ge(fetched[u], 16 * turn + 16)
                for q in range(2):
                    pe.wait_ge(copied, 2 * n + q + 3)
                    for k in range(4):
                        kk = 4 * q + k
                        last = nc.tensor.transpose([A0, A1][q][:, k * P:(k + 1) * P],
                                                   xe[u][:, :].rearrange("p (c k) -> p k c", k=KC)[:, kk, :], ident[:, :])
                    last.then_inc(turned, 1)

            def up(n, turn, u, bank, w, came):
                pe.wait_ge(came[u], 16 * turn + 16)
                pe.wait_ge(copied, 2 * n + 6)
                pe.wait_ge(multiplied, n + 1)
                for k in range(KC):
                    last = nc.tensor.matmul(bank[:, :], xeT[u][:, k, :], w[u][:, k, :],
                                            start=(k == 0), stop=(k == KC - 1))
                last.then_inc(hidden, 1)

            def turn_h(n, turn, u):
                pe.wait_ge(multiplied, n + 2)
                pe.wait_ge(hcopied, n + 1)
                for k in range(4):
                    last = nc.tensor.transpose(TB[:, k * P:(k + 1) * P],
                                               gl[u][:, :].rearrange("p (c k) -> p k c", k=4)[:, k, :], ident[:, :])
                last.then_inc(hturned, 1)

            def down(n, turn, u):
                pe.wait_ge(din_[u], 16 * turn + 16)
                pe.wait_ge(hcopied, n + 2)
                pe.wait_ge(read, n + 1)
                for half in range(2):
                    for k in range(4):
                        last = nc.tensor.matmul([Z0, Z1][half][:, :], hT[u][:, k, :],
                                                wd[u][:, k, half * 512:half * 512 + 512], start=(k == 0), stop=(k == 3))
                last.then_inc(downed, 1)

            def head(*b):
                turn_x(*b)
                up(*b, PA, wg, gin_)
                up(*b, PB, wu, uin_)
                turn_x(*succ(*b))

            def step(*b, more=True):
                up(*b, PA, wg, gin_)
                turn_h(*prev(*b))
                up(*b, PB, wu, uin_)
                down(*prev(*b))
                if more:
                    turn_x(*succ(*b))

            def tail(*b):
                turn_h(*b)
                down(*b)
            head(0, 0, 0)
            with pe.Fori(0, NE // 2 - 1) as i:
                step(i * 2 + 1, i, 1)
                step(i * 2 + 2, i + 1, 0)
            step(NE - 1, NE // 2 - 1, 1, more=False)
            tail(NE - 1, NE // 2 - 1, 1)

            def body(n, turn, u, e):
                turn_x(n, turn, u)
                up(n, turn, u, PA, wg, gin_)
                up(n, turn, u, PB, wu, uin_)
                turn_h(n, turn, u)
                down(n, turn, u)
            further(pe, body)

        @block.scalar
        def _(act):
            act.sem_inc(read, 1)
            act.sem_inc(s0, 16)
            act.sem_inc(s1, 16)

            def silu(n, turn, u):
                act.wait_ge(hidden, 2 * n + 5)
                nc.scalar.activation(gl[u][:, :], PA[:, :], ACT.Silu).then_inc(silued, 1)

            def out(n, turn, u):
                act.wait_ge(stored[u], 16 * turn + 16)
                act.wait_ge(downed, n + 3)
                for half in range(2):
                    last = nc.scalar.activation(ye[u][:, half * 512:half * 512 + 512], [Z0, Z1][half][:, :], ACT.Copy)
                last.then_inc(read, 1)
                act.wait_ge(read, n + 2)
                act.sem_inc(passed, 1)
                act.dma_start(ysd[bass.ds(n * P, P), :], ye[u][:, :]).then_inc(stored[u], 16)

            def step(*b):
                silu(*b)
                out(*prev(*b))
            piped(act, silu, step, out)

            def body(n, turn, u, e):
                silu(n, turn, u)
                out(n, turn, u)
            further(act, body)
            many = act.value_load(ovi[0:1, OVER:OVER + 1], min_val=0, max_val=OVER)
            act.wait_ge(s0, 16 + 16 * (NE // 2))
            act.wait_ge(s1, 16 + 16 * (NE // 2))
            with act.If(many > 0):
                with act.Fori(0, OVER // 2) as i:
                    for u in range(2):
                        with act.If(many > i * 2 + u):
                            act.wait_ge(stored[u], 16 * (NE // 2 + i) + 32)
                            act.sem_inc(passed, 1)

        @block.vector
        def _(ve):
            ve.wait_ge(toks_in, 16)
            nc.vector.tensor_copy(tflt[:, :], trows[:, :]).then_inc(named, 1)
            ve.wait_ge(hturned, 1)
            nc.vector.tensor_copy(toks[:, :], TB[:, 0:NB]).then_inc(named, 1)
            ve.sem_inc(copied, 4)
            ve.sem_inc(hcopied, 1)
            ve.sem_inc(multiplied, 1)

            def copy_x(n, turn, u):
                for q in range(2):
                    ve.wait_ge(turned, 2 * n + q + 1)
                    nc.vector.tensor_copy(xeT[u][:, 4 * q:4 * q + 4, :].rearrange("p a b -> p (a b)"),
                                          [A0, A1][q][:, :]).then_inc(copied, 1)

            def multiply(n, turn, u):
                ve.wait_ge(hidden, 2 * n + 6)
                ve.wait_ge(silued, n + 1)
                nc.vector.tensor_tensor(gl[u][:, :], gl[u][:, :], PB[:, :], ALU.mult).then_inc(multiplied, 1)

            def copy_h(n, turn, u):
                ve.wait_ge(hturned, n + 2)
                nc.vector.tensor_copy(hT[u][:, :, :].rearrange("p a b -> p (a b)"), TB[:, :]).then_inc(hcopied, 1)

            def head(*b):
                copy_x(*b)
                multiply(*b)
                copy_x(*succ(*b))

            def step(*b, more=True):
                copy_h(*prev(*b))
                multiply(*b)
                if more:
                    copy_x(*succ(*b))
            head(0, 0, 0)
            with ve.Fori(0, NE // 2 - 1) as i:
                step(i * 2 + 1, i, 1)
                step(i * 2 + 2, i + 1, 0)
            step(NE - 1, NE // 2 - 1, 1, more=False)
            copy_h(NE - 1, NE // 2 - 1, 1)

            def body(n, turn, u, e):
                copy_x(n, turn, u)
                multiply(n, turn, u)
                copy_h(n, turn, u)
            further(ve, body)

    ya = [at("ya", [P, D], F32, 8192 * i) for i in range(NT)]
    yb = [at("yb", [P, D], F32, 8192 * i + 4096) for i in range(NT)]
    f = 8192 * NT
    yo = [at("yo", [P, D], F32, f + 4096 * i) for i in range(3)]
    gf = at("gf", [P, D], F32, f + 12288)
    junk = at("junk", [P, D], F32, f + 16384)
    with Stage(nc) as ctx:
        g_in, summed, sq_done, inverted, rooted, finished, o0, o1, o2_, *ys_ = sems(
            ctx, "z", "g_in summed sq_done inverted rooted finished o0 o1 o2 " + " ".join(f"y{t}" for t in range(NT)))
        os_ = [o0, o1, o2_]
        block = ctx.enter_context(nc.Block())
        yp = io["out0"].rearrange("b t d -> (b t) d")
        ysm = io["out1"].rearrange("b t d -> (b t) d")

        @block.sync
        def _(sp):
            sp.dma_start(gf[:, :], io["norm_final"].partition_broadcast(P)).then_inc(g_in, 16)
            for t in range(NT):
                r = rows_of(t)
                sp.wait_ge(finished, t + 1)
                sp.dma_start(yp[t * P:t * P + r, :] if t < FULL else ysm[:, :],
                             yo[t % 3][0:r, :]).then_inc(os_[t % 3], 16)
            for i in range(3):
                sp.wait_ge(os_[i], 16 * (NT // 3))

        @block.gpsimd
        def _(pool):
            for t in range(NT):
                r = rows_of(t)
                for k, dst in enumerate((ya, yb)):
                    pool.indirect_dma_start(dst[t][0:r, :], None, ysd,
                                            bass.IndirectOffsetOnAxis(ap=sidx[k][0:r, t:t + 1], axis=0)).then_inc(ys_[t], 16)

        @block.scalar
        def _(act):
            for t in range(NT):
                r = rows_of(t)
                act.wait_ge(summed, t + 1)
                nc.scalar.activation(junk[0:r, :], ya[t][0:r, :], ACT.Square, scale=D ** -0.5,
                                     accum_out=stat[0:r, t:t + 1]).then_inc(sq_done, 1)
                act.wait_ge(inverted, t + 1)
                nc.scalar.activation(stat[0:r, 32 + t:33 + t], stat[0:r, 16 + t:17 + t], ACT.Sqrt).then_inc(rooted, 1)

        @block.vector
        def _(ve):
            def add(t):
                r = rows_of(t)
                ve.wait_ge(ys_[t], 32)
                nc.vector.scalar_tensor_tensor(out=wide(ya[t][0:r, :]), in0=wide(ya[t][0:r, :]), scalar=wts[0:r, t, 0:1],
                                               in1=hrow(t, r), op0=ALU.mult, op1=ALU.add)
                ve.drain()
                nc.vector.scalar_tensor_tensor(out=ya[t][0:r, :], in0=yb[t][0:r, :], scalar=wts[0:r, t, 1:2],
                                               in1=ya[t][0:r, :], op0=ALU.mult, op1=ALU.add).then_inc(summed, 1)

            def scale(t):
                r = rows_of(t)
                ve.wait_ge(sq_done, t + 1)
                nc.vector.tensor_scalar(stat[0:r, 16 + t:17 + t], stat[0:r, t:t + 1], EPS, None, ALU.add)
                ve.drain()
                nc.vector.reciprocal(stat[0:r, 16 + t:17 + t], stat[0:r, 16 + t:17 + t]).then_inc(inverted, 1)
                ve.wait_ge(rooted, t + 1)
                if t >= 3:
                    ve.wait_ge(os_[t % 3], 16 * (t // 3))
                nc.vector.scalar_tensor_tensor(out=yo[t % 3][0:r, :], in0=ya[t][0:r, :], scalar=stat[0:r, 32 + t:33 + t],
                                               in1=gf[0:r, :], op0=ALU.mult, op1=ALU.mult).then_inc(finished, 1)
            ve.wait_ge(g_in, 16)
            for t in range(NT + 1):
                if t < NT:
                    add(t)
                if t >= 1:
                    scale(t - 1)

    top.close()


_OUTS = [(1, 1024, 1024), (1, 64, 1024), (1, 1, 1024, 8, 64), (1, 1, 1024, 8, 64), (1, 1, 4, 64, 128),
         (1, 1, 256, 4, 128), (1, 1, 256, 4, 128), (1, 1, 64, 8, 64), (1, 1, 64, 8, 64), (1, 1, 4, 64, 128)]
_INS = ["x_prompt", "x_sample", "mem_prompt", "cache_sb_k", "cache_sb_v", "state_gla", "cache_mem_k", "cache_mem_v",
        "norm_mix", "w_in", "w_gla_a2", "b_gla_a", "gla_norm", "norm_mem", "w_mem_kv", "w_branch", "w_out",
        "norm_ffn", "w_coarse", "b_coarse", "w_fine", "b_fine", "w_e_gate", "w_e_up", "w_e_down", "norm_final"]


def kernel(**inputs):
    import numpy as _np
    import concourse.bacc as _bacc
    from concourse import mybir as _mybir
    from concourse.bass_utils import run_bass_kernel_spmd as _run

    nc = _bacc.Bacc("TRN2", target_bir_lowering=False, num_devices=1)
    arrays, io = {}, {}
    for name in _INS:
        a = _np.ascontiguousarray(inputs[name])
        arrays[f"in_{name}_dram"] = a
        io[name] = nc.dram_tensor(f"in_{name}_dram", a.shape, _mybir.dt.from_np(a.dtype), kind="ExternalInput").ap()
    for i, shape in enumerate(_OUTS):
        io[f"out{i}"] = nc.dram_tensor(f"out_{i}_dram", shape, _mybir.dt.float32, kind="ExternalOutput").ap()
    build(nc, io)
    r = _run(nc, [arrays], core_ids=[0])
    return tuple(r.results[0][f"out_{i}_dram"] for i in range(len(_OUTS)))
```
